# Optimizing a Trainium2 kernel written in Bass

```python
import jax, jax.numpy as jnp
from jax import lax
import numpy as np

D_MODEL = 1024
BATCH = 1
SEQ = 4096
DEPTH = 1

CHUNK = 64
N_MIXERS = 4
HEAD_DIM = 64
W_MIX = D_MODEL
N_HEADS = W_MIX // HEAD_DIM
N_KV_HEADS = 4
KV_W = N_KV_HEADS * HEAD_DIM
SWA_WINDOW = 128
SWA_PREV_CHUNKS = SWA_WINDOW // CHUNK - 1
CHUNK_PREV = 8
REL_CLIP = 128
CONV_WIDTH = 3
N_MEM = 256
MEM_HEADS = 4
MEM_HEAD_DIM = 128
MEM_W = MEM_HEADS * MEM_HEAD_DIM
BRANCH_W = W_MIX + MEM_W
DECAY_LORA = 64
ICLR_LORA = 64
RWKV_HEADS = N_HEADS
RWKV_HEAD_DIM = HEAD_DIM
GN_EPS = 64e-5
NORM_EPS = 1e-6
NEG_INF = -1e30
P_A = 3 * W_MIX
P_B = W_MIX + 2 * KV_W
P_C = 3 * W_MIX
P_D = 3 * W_MIX + DECAY_LORA + ICLR_LORA
P_MIX = (P_A, P_B, P_C, P_D)

kernel_name = 'interleaved_chunk_causal_hybrid_trunk'

def _n_of(m):
    return len(range(m, DEPTH, N_MIXERS))

def rms_norm(x, g):
    xf = x.astype(jnp.float32)
    y = xf * lax.rsqrt(jnp.mean(xf * xf, axis=-1, keepdims=True) + NORM_EPS)
    return (y * g.astype(jnp.float32)).astype(x.dtype)

def alibi_slopes(n):
    return jnp.power(2.0, -8.0 * jnp.arange(1, n + 1, dtype=jnp.float32) / n)

def _chunk_rel(n_prev):
    band = (n_prev + 1) * CHUNK
    return (jnp.arange(CHUNK)[:, None] + n_prev * CHUNK) - jnp.arange(band)[None, :]

def banded_chunk_attention(q, k, v, n_prev, bias, sinks=None):
    bsz, seq, n_h, hd = q.shape
    n_kv = k.shape[2]
    grp = n_h // n_kv
    n_chunks = seq // CHUNK
    band = (n_prev + 1) * CHUNK
    pad = n_prev * CHUNK
    kp = jnp.pad(k, ((0, 0), (pad, 0), (0, 0), (0, 0)))
    vp = jnp.pad(v, ((0, 0), (pad, 0), (0, 0), (0, 0)))
    qc = q.reshape(bsz, n_chunks, CHUNK, n_kv, grp, hd).transpose(1, 0, 2, 3, 4, 5)
    bias_g = bias.reshape(n_kv, grp, CHUNK, band)
    key_off = jnp.arange(band) - pad
    scale = hd ** -0.5
    if sinks is not None:
        sink = sinks.astype(jnp.float32).reshape(1, n_kv, grp, 1, 1)

    def one_chunk(args):
        c, qb = args
        kb = lax.dynamic_slice_in_dim(kp, c * CHUNK, band, axis=1)
        vb = lax.dynamic_slice_in_dim(vp, c * CHUNK, band, axis=1)
        s = jnp.einsum('btkgd,bskd->bkgts', qb, kb).astype(jnp.float32) * scale + bias_g
        s = jnp.where((c * CHUNK + key_off) >= 0, s, NEG_INF)
        if sinks is None:
            p = jax.nn.softmax(s, axis=-1)
        else:
            mx = jnp.maximum(jnp.max(s, axis=-1, keepdims=True), sink)
            e = jnp.exp(s - mx)
            p = e / (jnp.sum(e, axis=-1, keepdims=True) + jnp.exp(sink - mx))
        return jnp.einsum('bkgts,bskd->btkgd', p.astype(vb.dtype), vb)

    out = lax.map(one_chunk, (jnp.arange(n_chunks), qc))
    return out.transpose(1, 0, 2, 3, 4, 5).reshape(bsz, seq, n_h * hd)

def short_conv_mixer(p, conv_w):
    b_gate, c_gate, u = jnp.split(p, 3, axis=-1)
    z = c_gate * u
    seq = z.shape[1]
    zp = jnp.pad(z, ((0, 0), (CONV_WIDTH - 1, 0), (0, 0)))
    y = conv_w[0] * zp[:, 0:seq]
    for j in range(1, CONV_WIDTH):
        y = y + conv_w[j] * zp[:, j:j + seq]
    return b_gate * y

def swa_sink_mixer(p, sinks):
    bsz, seq, _ = p.shape
    q = p[..., :W_MIX].reshape(bsz, seq, N_HEADS, HEAD_DIM)
    k = p[..., W_MIX:W_MIX + KV_W].reshape(bsz, seq, N_KV_HEADS, HEAD_DIM)
    v = p[..., W_MIX + KV_W:].reshape(bsz, seq, N_KV_HEADS, HEAD_DIM)
    rel = _chunk_rel(SWA_PREV_CHUNKS)
    bias = -alibi_slopes(N_HEADS)[:, None, None] * jnp.abs(rel).astype(jnp.float32)[None]
    return banded_chunk_attention(q, k, v, SWA_PREV_CHUNKS, bias, sinks)

def chunk_relpos_mixer(p, table):
    bsz, seq, _ = p.shape
    q, k, v = [t.reshape(bsz, seq, N_HEADS, HEAD_DIM) for t in jnp.split(p, 3, axis=-1)]
    rel = _chunk_rel(CHUNK_PREV)
    bias = table[:, jnp.clip(rel, -REL_CLIP, REL_CLIP) + REL_CLIP].astype(jnp.float32)
    return banded_chunk_attention(q, k, v, CHUNK_PREV, bias)

def rwkv7_scan(r, w, k, v, kk, a):
    bsz, _, n_h, n = r.shape

    def step(S, inp):
        r_t, w_t, k_t, v_t, kk_t, a_t = inp
        s_kk = jnp.einsum('bhvk,bhk->bhv', S, kk_t)
        S = (S * w_t[:, :, None, :] - s_kk[..., None] * (kk_t * a_t)[:, :, None, :]
             + v_t[..., None] * k_t[:, :, None, :])
        return S, jnp.einsum('bhvk,bhk->bhv', S, r_t)

    xs = [t.transpose(1, 0, 2, 3) for t in (r, w, k, v, kk, a)]
    s0 = jnp.zeros((bsz, n_h, n, n), jnp.float32)
    _, o = lax.scan(step, s0, xs)
    return o.transpose(1, 0, 2, 3)

def rwkv7_mixer(p, mu, w0, w2, a0, a2, k_k, k_a, r_k, ln_w, ln_b):
    dt = p.dtype
    bsz, seq, _ = p.shape
    f32 = jnp.float32
    hs = (RWKV_HEADS, RWKV_HEAD_DIM)
    p_prev = jnp.pad(p, ((0, 0), (1, 0), (0, 0)))[:, :-1]
    p = p + mu * (p_prev - p)
    r, k, v = p[..., :W_MIX], p[..., W_MIX:2 * W_MIX], p[..., 2 * W_MIX:3 * W_MIX]
    wl = p[..., 3 * W_MIX:3 * W_MIX + DECAY_LORA]
    al = p[..., 3 * W_MIX + DECAY_LORA:]
    w = -jax.nn.softplus(-(w0 + jnp.tanh(wl) @ w2).astype(f32)) - 0.5
    decay = jnp.exp(-jnp.exp(w))
    a = jax.nn.sigmoid((a0 + al @ a2).astype(f32))
    shp = (bsz, seq) + hs
    r, k, v = r.astype(f32).reshape(shp), k.astype(f32).reshape(shp), v.astype(f32).reshape(shp)
    decay, a = decay.reshape(shp), a.reshape(shp)
    kk = k * k_k.astype(f32).reshape(hs)
    kk = kk / jnp.maximum(jnp.sqrt(jnp.sum(kk * kk, axis=-1, keepdims=True)), 1e-12)
    k = k * (1.0 + (a - 1.0) * k_a.astype(f32).reshape(hs))
    o = rwkv7_scan(r, decay, k, v, kk, a)
    mean = jnp.mean(o, axis=-1, keepdims=True)
    var = jnp.mean(jnp.square(o - mean), axis=-1, keepdims=True)
    o = (o - mean) * lax.rsqrt(var + GN_EPS) * ln_w.astype(f32).reshape(hs) + ln_b.astype(f32).reshape(hs)
    o = o + jnp.sum(r * k * r_k.astype(f32).reshape(hs), axis=-1, keepdims=True) * v
    return o.reshape(bsz, seq, W_MIX).astype(dt)

def memory_cross_attention(q_p, mem, mem_g, w_kv):
    bsz, seq, _ = q_p.shape
    n_mem = mem.shape[1]
    kv = rms_norm(mem, mem_g) @ w_kv
    k = kv[..., :MEM_W].reshape(bsz, n_mem, MEM_HEADS, MEM_HEAD_DIM)
    v = kv[..., MEM_W:].reshape(bsz, n_mem, MEM_HEADS, MEM_HEAD_DIM)
    q = q_p.reshape(bsz, seq, MEM_HEADS, MEM_HEAD_DIM)
    s = jnp.einsum('bthd,bmhd->bhtm', q, k).astype(jnp.float32) * (MEM_HEAD_DIM ** -0.5)
    p = jax.nn.softmax(s, axis=-1)
    o = jnp.einsum('bhtm,bmhd->bthd', p.astype(v.dtype), v)
    return o.reshape(bsz, seq, MEM_W)

def setup_inputs(seed: int = 0) -> dict:
    key = jax.random.key(seed)
    ks = jax.random.split(key, 26)
    f32 = jnp.float32

    def nrm(k, shape, scale):
        return jax.random.normal(k, shape, f32) * scale

    n_a, n_b, n_c, n_d = _n_of(0), _n_of(1), _n_of(2), _n_of(3)
    extra = BRANCH_W + MEM_W
    return {
        'x': nrm(ks[0], (BATCH, SEQ, D_MODEL), 1.0),
        'mem': nrm(ks[1], (BATCH, N_MEM, D_MODEL), 1.0),
        'pre_norm': 1.0 + nrm(ks[2], (DEPTH, D_MODEL), 0.1),
        'post_norm': 1.0 + nrm(ks[3], (DEPTH, D_MODEL), 0.1),
        'mem_norm': 1.0 + nrm(ks[4], (DEPTH, D_MODEL), 0.1),
        'w_mem_kv': nrm(ks[5], (DEPTH, D_MODEL, 2 * MEM_W), D_MODEL ** -0.5),
        'w_out': nrm(ks[6], (DEPTH, BRANCH_W, D_MODEL), BRANCH_W ** -0.5),
        'w_in_a': nrm(ks[7], (n_a, D_MODEL, P_A + extra), D_MODEL ** -0.5),
        'conv_a': nrm(ks[8], (n_a, CONV_WIDTH, W_MIX), CONV_WIDTH ** -0.5),
        'w_in_b': nrm(ks[9], (n_b, D_MODEL, P_B + extra), D_MODEL ** -0.5),
        'sinks_b': nrm(ks[10], (n_b, N_HEADS), 1.0),
        'w_in_c': nrm(ks[11], (n_c, D_MODEL, P_C + extra), D_MODEL ** -0.5),
        'relbias_c': nrm(ks[12], (n_c, N_HEADS, 2 * REL_CLIP + 1), 0.5),
        'w_in_d': nrm(ks[13], (n_d, D_MODEL, P_D + extra), D_MODEL ** -0.5),
        'mu_d': jax.random.uniform(ks[14], (n_d, P_D), f32, 0.0, 1.0),
        'w0_d': jax.random.uniform(ks[15], (n_d, W_MIX), f32, -2.0, 4.0),
        'w2_d': nrm(ks[16], (n_d, DECAY_LORA, W_MIX), DECAY_LORA ** -0.5),
        'a0_d': nrm(ks[17], (n_d, W_MIX), 0.5),
        'a2_d': nrm(ks[18], (n_d, ICLR_LORA, W_MIX), ICLR_LORA ** -0.5),
        'kk_d': 0.85 + nrm(ks[19], (n_d, W_MIX), 0.1),
        'ka_d': 1.0 + nrm(ks[20], (n_d, W_MIX), 0.1),
        'rk_d': nrm(ks[21], (n_d, W_MIX), 0.1),
        'lnw_d': 1.0 + nrm(ks[22], (n_d, W_MIX), 0.1),
        'lnb_d': nrm(ks[23], (n_d, W_MIX), 0.02),
    }

def reference(x, mem, pre_norm, post_norm, mem_norm, w_mem_kv, w_out, w_in_a, conv_a,
              w_in_b, sinks_b, w_in_c, relbias_c, w_in_d, mu_d, w0_d, w2_d, a0_d, a2_d,
              kk_d, ka_d, rk_d, lnw_d, lnb_d):
    w_in = (w_in_a, w_in_b, w_in_c, w_in_d)
    for i in range(DEPTH):
        m, j = i % N_MIXERS, i // N_MIXERS
        h = rms_norm(x, pre_norm[i])
        proj = h @ w_in[m][j]
        pm = P_MIX[m]
        p = proj[..., :pm]
        gate = proj[..., pm:pm + BRANCH_W]
        mq = proj[..., pm + BRANCH_W:]
        if m == 0:
            mix = short_conv_mixer(p, conv_a[j])
        elif m == 1:
            mix = swa_sink_mixer(p, sinks_b[j])
        elif m == 2:
            mix = chunk_relpos_mixer(p, relbias_c[j])
        else:
            mix = rwkv7_mixer(p, mu_d[j], w0_d[j], w2_d[j], a0_d[j], a2_d[j],
                              kk_d[j], ka_d[j], rk_d[j], lnw_d[j], lnb_d[j])
        mem_o = memory_cross_attention(mq, mem, mem_norm[i], w_mem_kv[i])
        y = (jnp.concatenate([mix, mem_o], axis=-1) * jax.nn.silu(gate)) @ w_out[i]
        x = x + rms_norm(y, post_norm[i])
    return x


_drawn_inputs = setup_inputs


def setup_inputs(seed=0):
    import zlib

    import numpy as np

    out = dict(_drawn_inputs(seed))
    spreads = {}
    factors = {'mem_norm': 7.083}
    for name, (base, spread) in spreads.items():
        noise = np.random.default_rng([zlib.crc32(name.encode()), seed]).standard_normal(out[name].shape)
        drawn = base * np.exp(spread * noise) if base else spread * noise
        out[name] = __import__('jax').numpy.asarray(drawn.astype(out[name].dtype))
    for name, factor in factors.items():
        out[name] = (out[name] * factor).astype(out[name].dtype)
    return out
```

```python
from contextlib import ExitStack

import concourse.bass as bass
from concourse import mybir

P = 128
D = 1024
SEQ = 4096
TILE = 512
NT = SEQ // TILE
SUB = TILE // P
KT = D // P
CH = D // P
CONV = 3
HALO = CONV - 1
MH = 4
HD = 128
NM = 256
MT = NM // P
BR = D + MH * HD
BT = BR // P
HALF = 512
BLOCK = 1024
NKV = 2 * MH * HD * D // (P * BLOCK)
HEAD_BLOCKS = 2 + 2 * 4
PAIR_BLOCKS = 2 * HEAD_BLOCKS
IN_BLOCKS = MH * HEAD_BLOCKS
OUT_BLOCKS = BT * D // BLOCK
TILE_BLOCKS = IN_BLOCKS + OUT_BLOCKS
AHEAD = 3
RAW = 2
RING = AHEAD + 1
RES = 3
EPS = 1e-6
SCALE = HD ** -0.5
CREDIT = 1
Q, C0, U0, B0, G0, C1, U1, B1, G1, MG = range(HEAD_BLOCKS)


def trunk(nc, x, mem, pre_g, post_g, mem_g, conv, blocks, out):
    f32 = mybir.dt.float32
    f32r = mybir.dt.float32r
    bf16 = mybir.dt.bfloat16
    ALU = mybir.AluOpType
    ACT = mybir.ActivationFunctionType
    AX = mybir.AxisListType
    ds = bass.ds

    with ExitStack() as ctx:
        def sb(name, shape, dt=f32):
            return ctx.enter_context(nc.sbuf_tensor(name, [P] + list(shape), dt))

        def sem(name):
            return ctx.enter_context(nc.semaphore(name))

        w_raw = sb("w_raw", [RAW, BLOCK])
        w_hi = sb("w_hi", [RING, BLOCK], f32r)
        w_lo = sb("w_lo", [RING, BLOCK], f32r)
        h_hi = sb("h_hi", [KT, TILE], f32r)
        h_lo = sb("h_lo", [KT, TILE], f32r)
        g_hi = sb("g_hi", [BT, TILE], f32r)
        g_lo = sb("g_lo", [BT, TILE], f32r)
        k_hi = sb("k_hi", [MH, NM], f32r)
        k_lo = sb("k_lo", [MH, NM], f32r)
        v_hi = sb("v_hi", [MT, MH * HD], f32r)
        v_lo = sb("v_lo", [MT, MH * HD], f32r)
        vh_hi = sb("vh_hi", [MT, HD], f32r)
        vh_lo = sb("vh_lo", [MT, HD], f32r)
        q_hi = sb("q_hi", [TILE], f32r)
        q_lo = sb("q_lo", [TILE], f32r)
        pt_hi = sb("pt_hi", [MT, TILE], f32r)
        pt_lo = sb("pt_lo", [MT, TILE], f32r)
        x_in = sb("x_in", [SUB, D])
        x_res = sb("x_res", [RES, D])
        pre_gain = sb("pre_gain", [D])
        post_gain = sb("post_gain", [D])
        y_left = sb("y_left", [SUB, HALF])
        probs = y_left[:, 0:2, :].rearrange("p a (b m) -> p (a b) m", b=2)
        mem_gain = y_left[:, 2:4, :].rearrange("p a b -> p (a b)")
        conv_w = sb("conv_w", [CH, CONV])
        z_halo = sb("z_halo", [CH, HALO])
        z = sb("z", [HALO + TILE])
        c_sb = sb("c_sb", [TILE])
        mix = sb("mix", [TILE])
        silu = sb("silu", [TILE])
        junk = sb("junk", [D], bf16)
        ident = sb("ident", [P])
        eps = sb("eps", [1])
        sq = sb("sq", [SUB])
        sd = sb("sd", [SUB])
        rs = sb("rs", [SUB])
        ysq = sb("ysq", [2, SUB])
        yss = sb("yss", [SUB])
        ysd = sb("ysd", [SUB])
        yrs = sb("yrs", [SUB])
        rmax = sb("rmax", [SUB])
        nmax = sb("nmax", [SUB])
        rsum = sb("rsum", [SUB])
        rinv = sb("rinv", [SUB])

        psum = ctx.enter_context(nc.psum_tensor("banks", [P, 8, HALF], f32))
        scores = psum[:, 4:6, :].rearrange("p a (b m) -> p (a b) m", b=2)
        probs_t = psum[:, 6:8, :]
        mem_o = psum[:, 4, :]

        def turned(s):
            return psum[:, 4 + 2 * (s % 2):6 + 2 * (s % 2), :].rearrange("p a (b n) -> p (a b) n", b=4)

        w_in_dma = [sem(f"w_in_dma{i}") for i in range(RAW)]
        x_in_dma = [sem(f"x_in_dma{i}") for i in range(SUB)]
        x_res_dma = [sem(f"x_res_dma{i}") for i in range(RES)]
        out_dma = [sem(f"out_dma{i}") for i in range(RES)]
        gain_dma = sem("gain_dma")
        consts_set = sem("consts_set")
        pool_passed = sem("pool_passed")
        w_hi_done = sem("w_hi_done")
        w_lo_done = sem("w_lo_done")
        blocks_done = sem("blocks_done")
        sq_done = sem("sq_done")
        sd_done = sem("sd_done")
        rs_done = sem("rs_done")
        rows_normed = sem("rows_normed")
        rows_turned = sem("rows_turned")
        rows_hi = sem("rows_hi")
        rows_lo = sem("rows_lo")
        kv_hi_done = sem("kv_hi_done")
        kv_lo_done = sem("kv_lo_done")
        vh_done = sem("vh_done")
        q_hi_done = sem("q_hi_done")
        q_lo_done = sem("q_lo_done")
        scores_done = sem("scores_done")
        rmax_done = sem("rmax_done")
        nmax_done = sem("nmax_done")
        exp_done = sem("exp_done")
        rinv_done = sem("rinv_done")
        probs_done = sem("probs_done")
        turned_done = sem("turned_done")
        pt_hi_done = sem("pt_hi_done")
        pt_lo_done = sem("pt_lo_done")
        pv_done = sem("pv_done")
        c_done = sem("c_done")
        halo_in = sem("halo_in")
        z_done = sem("z_done")
        halo_out = sem("halo_out")
        tap2_done = sem("tap2_done")
        tap1_done = sem("tap1_done")
        tap0_done = sem("tap0_done")
        b_used = sem("b_used")
        silu_done = sem("silu_done")
        gated = sem("gated")
        g_hi_done = sem("g_hi_done")
        g_lo_done = sem("g_lo_done")
        y_left_done = sem("y_left_done")
        y_right_done = sem("y_right_done")
        ysq_done = sem("ysq_done")
        yss_done = sem("yss_done")
        ysd_done = sem("ysd_done")
        yrs_done = sem("yrs_done")
        y_scaled = sem("y_scaled")
        y_final = sem("y_final")

        block = ctx.enter_context(nc.Block())

        def per_tile(i):
            return len(range(i, SUB, RES))

        def flat(ap):
            return ap.rearrange("p a b -> p (a b)")

        @block.sync
        def _(sp):
            def load(m, slot, src):
                sp.dma_start(w_raw[:, slot, :], src).then_inc(w_in_dma[slot], 16)

            for m in range(NKV):
                if m >= RAW:
                    sp.wait_ge(w_lo_done, m - RAW + 1)
                load(m, m % RAW, blocks[m])
            with sp.Fori(0, NT) as t:
                with sp.Fori(0, TILE_BLOCKS // RAW) as pair:
                    for i in range(RAW):
                        m = NKV + t * TILE_BLOCKS + pair * RAW + i
                        sp.wait_ge(w_lo_done, m - RAW + 1)
                        src = blocks[ds(NKV + pair * RAW + i, 1), :, :].rearrange("a p n -> p (a n)")
                        load(m, i, src)

        @block.gpsimd
        def _(pool):
            pool.dma_start(x_res[:, 0, :], mem[0:P, :]).then_inc(x_res_dma[0], 16)
            pool.dma_start(x_res[:, 1, :], mem[P:2 * P, :]).then_inc(x_res_dma[1], 16)
            pool.dma_start(mem_gain, mem_g).then_inc(gain_dma, 16)
            for s in range(SUB):
                pool.dma_start(x_in[:, s, :], x[s * P:(s + 1) * P, :]).then_inc(x_in_dma[s], 16)
            pool.dma_start(pre_gain[:], pre_g).then_inc(gain_dma, 16)
            pool.dma_start(post_gain[:], post_g).then_inc(gain_dma, 16)
            pool.dma_start(conv_w[:], conv).then_inc(gain_dma, 16)
            pool.memset(ident[:], 0.0).then_inc(consts_set, 1)
            pool.memset(eps[:], EPS).then_inc(consts_set, 1)
            pool.memset(z_halo[:], 0.0).then_inc(consts_set, 1)
            pool.wait_ge(consts_set, 3)
            pool.affine_select(out=ident[:], in_=ident[:], compare_op=ALU.not_equal, fill=1.0, base=0,
                               pattern=[[-1, P]], channel_multiplier=1).then_inc(consts_set, 1)

            def load_residual(t, s):
                pool.dma_start(x_res[:, s % RES, :], x[ds((t * SUB + s) * P, P), :]).then_inc(x_res_dma[s % RES], 16)

            def tile(t, more):
                for s in range(RES):
                    load_residual(t, s)
                if more:
                    for s in range(SUB):
                        pool.wait_ge(rows_turned, MT + t * SUB + s + 1)
                        pool.sem_inc(pool_passed, 1)
                        pool.dma_start(x_in[:, s, :], x[ds(((t + 1) * SUB + s) * P, P), :]).then_inc(x_in_dma[s], 16)
                for s in range(SUB):
                    pool.wait_ge(y_final, CREDIT + t * SUB + s + 1)
                    pool.sem_inc(pool_passed, 1)
                    pool.dma_start(out[ds((t * SUB + s) * P, P), :], x_res[:, s % RES, :]).then_inc(out_dma[s % RES], 16)
                    if s + RES < SUB:
                        pool.wait_ge(out_dma[s], (t * 2 + 1) * 16)
                        pool.sem_inc(pool_passed, 1)
                        load_residual(t, s + RES)
                for i in range(RES):
                    pool.wait_ge(out_dma[i], (t + 1) * per_tile(i) * 16)

            pool.wait_ge(rows_turned, MT)
            with pool.Fori(0, NT - 1) as t:
                tile(t, True)
            tile(NT - 1, False)

        @block.scalar
        def _(act):
            def hi_of(m_half, m, slot):
                act.wait_ge(w_in_dma[slot % RAW], (m_half + 1) * 16)
                act.wait_ge(blocks_done, m - RING + 1)
                nc.scalar.activation(w_hi[:, slot, :], w_raw[:, slot % RAW, :], ACT.Copy).then_inc(w_hi_done, 1)

            def rows_hi_of(r, s, dst):
                act.wait_ge(rows_turned, r + 1)
                nc.scalar.activation(dst, turned(s), ACT.Copy).then_inc(rows_hi, 1)

            act.sem_inc(silu_done, CREDIT)
            act.wait_ge(consts_set, 4)
            sq_n = 0
            for s in range(MT):
                act.wait_ge(x_res_dma[s], 16)
                if sq_n:
                    act.wait_ge(sq_done, sq_n)
                nc.scalar.activation(junk[:], x_res[:, s, :], ACT.Square, accum_out=sq[:, s:s + 1]).then_inc(sq_done, 1)
                sq_n += 1
            act.wait_ge(sq_done, sq_n)
            nc.scalar.activation(sd[:, 0:MT], sq[:, 0:MT], ACT.Sqrt, scale=1.0 / D, bias=eps[:]).then_inc(sd_done, 1)
            for m in range(AHEAD):
                act.wait_ge(w_in_dma[m % RAW], (m // RAW + 1) * 16)
                nc.scalar.activation(w_hi[:, m, :], w_raw[:, m % RAW, :], ACT.Copy).then_inc(w_hi_done, 1)
            for s in range(MT):
                rows_hi_of(s, s, g_hi[:, 0:KT, s * P:(s + 1) * P])
            act.wait_ge(rs_done, 1)
            for s in range(SUB):
                act.wait_ge(x_in_dma[s], 16)
                act.wait_ge(sq_done, sq_n)
                nc.scalar.activation(junk[:], x_in[:, s, :], ACT.Square, accum_out=sq[:, s:s + 1]).then_inc(sq_done, 1)
                sq_n += 1
            act.wait_ge(sq_done, sq_n)
            nc.scalar.activation(sd[:], sq[:], ACT.Sqrt, scale=1.0 / D, bias=eps[:]).then_inc(sd_done, 1)
            for s in range(SUB):
                rows_hi_of(MT + s, s, h_hi[:, :, s * P:(s + 1) * P])
            for m in range(NKV):
                n = m + AHEAD
                act.wait_ge(w_in_dma[n % RAW], (n // RAW + 1) * 16)
                if n >= RING:
                    act.wait_ge(blocks_done, n - RING + 1)
                nc.scalar.activation(w_hi[:, n % RING, :], w_raw[:, n % RAW, :], ACT.Copy).then_inc(w_hi_done, 1)
                if 1 <= m <= MH:
                    act.wait_ge(blocks_done, m)
                    nc.scalar.activation(k_hi[:, m - 1, :], psum[:, m - 1, 0:NM], ACT.Copy).then_inc(kv_hi_done, 1)
            act.wait_ge(blocks_done, NKV)
            for m in range(MT):
                nc.scalar.activation(v_hi[:, m, :], psum[:, m, :], ACT.Copy).then_inc(kv_hi_done, 1)

            def head_step(t, hp, i):
                h = t * MH + hp * 2 + i
                j = h * 2
                n = NKV + t * TILE_BLOCKS + hp * PAIR_BLOCKS + i * HEAD_BLOCKS
                half = NKV // 2 + t * (TILE_BLOCKS // 2) + hp * (PAIR_BLOCKS // 2) + i * (HEAD_BLOCKS // 2)

                def ahead(p):
                    a = i * HEAD_BLOCKS + p + AHEAD
                    hi_of(half + (p + AHEAD) // 2, n + p + AHEAD, a % RING)

                def came(p):
                    act.wait_ge(blocks_done, n + p + 1)

                def gate(p, bank, jj, item):
                    came(p)
                    act.wait_ge(gated, CREDIT + h * 3 + item)
                    nc.scalar.activation(silu[:], psum[:, bank, :], ACT.Silu).then_inc(silu_done, 1)

                def hi_of_gated(item, dst):
                    act.wait_ge(gated, CREDIT + h * 3 + item + 1)
                    nc.scalar.activation(dst, mix[:], ACT.Copy).then_inc(g_hi_done, 1)

                ahead(Q)
                came(Q)
                nc.scalar.activation(q_hi[:], psum[:, 0, :], ACT.Copy).then_inc(q_hi_done, 1)
                ahead(C0)
                came(C0)
                act.wait_ge(z_done, CREDIT + j)
                nc.scalar.activation(c_sb[:], psum[:, 1, :], ACT.Copy).then_inc(c_done, 1)
                ahead(U0)
                ahead(B0)
                act.wait_ge(nmax_done, h + 1)
                if i == 0:
                    act.wait_ge(y_final, CREDIT + t * SUB)
                for s in range(SUB):
                    op = nc.scalar.activation(probs[:, s, :], scores[:, s, :], ACT.Exp, scale=SCALE,
                                              bias=nmax[:, s:s + 1], accum_out=rsum[:, s:s + 1])
                    op.then_inc(exp_done, 1)
                ahead(G0)
                gate(G0, 0, 0, 0)
                ahead(C1)
                act.wait_ge(turned_done, h + 1)
                nc.scalar.activation(flat(pt_hi[:]), flat(probs_t), ACT.Copy).then_inc(pt_hi_done, 1)
                hi_of_gated(0, flat(g_hi[:, ds(hp * 4 + i * 2, 1), :]))
                came(C1)
                act.wait_ge(z_done, CREDIT + j + 1)
                nc.scalar.activation(c_sb[:], psum[:, 1, :], ACT.Copy).then_inc(c_done, 1)
                ahead(U1)
                ahead(B1)
                ahead(G1)
                gate(G1, 0, 1, 1)
                ahead(MG)
                hi_of_gated(1, flat(g_hi[:, ds(hp * 4 + i * 2 + 1, 1), :]))
                gate(MG, 1, 2, 2)
                hi_of_gated(2, flat(g_hi[:, ds(hp * 2 + i + CH, 1), :]))

            def out_step(t, more):
                n = NKV + t * TILE_BLOCKS + IN_BLOCKS
                half = NKV // 2 + t * (TILE_BLOCKS // 2) + IN_BLOCKS // 2
                r = MT + (t + 1) * SUB
                if more:
                    for s in range(SUB):
                        act.wait_ge(x_in_dma[s], (t + 2) * 16)
                        act.wait_ge(sq_done, r + s)
                        nc.scalar.activation(junk[:], x_in[:, s, :], ACT.Square, accum_out=sq[:, s:s + 1]).then_inc(sq_done, 1)
                    act.wait_ge(sq_done, r + SUB)
                    nc.scalar.activation(sd[:], sq[:], ACT.Sqrt, scale=1.0 / D, bias=eps[:]).then_inc(sd_done, 1)
                for p in range(OUT_BLOCKS):
                    if more or p + AHEAD < OUT_BLOCKS:
                        hi_of(half + (p + AHEAD) // 2, n + p + AHEAD, (p + AHEAD) % RING)
                    if more and 2 <= p < 2 + SUB:
                        s = p - 2
                        rows_hi_of(r + s, s, h_hi[:, :, s * P:(s + 1) * P])
                    if p == OUT_BLOCKS // 2:
                        act.wait_ge(blocks_done, n + p)
                        for s in range(SUB):
                            nc.scalar.activation(y_left[:, s, :], psum[:, s, :], ACT.Copy).then_inc(y_left_done, 1)
                        for s in range(SUB):
                            act.wait_ge(ysq_done, t * 2 * SUB + s) if s else None
                            nc.scalar.activation(junk[:, 0:HALF], psum[:, s, :], ACT.Square,
                                                 accum_out=ysq[:, 0, s:s + 1]).then_inc(ysq_done, 1)
                for s in range(SUB):
                    if s < SUB - 1:
                        act.wait_ge(y_right_done, t * (SUB - 1) + s + 1)
                    else:
                        act.wait_ge(blocks_done, n + OUT_BLOCKS)
                    act.wait_ge(ysq_done, t * 2 * SUB + SUB + s)
                    nc.scalar.activation(junk[:, 0:HALF], psum[:, 4 + s, :], ACT.Square,
                                         accum_out=ysq[:, 1, s:s + 1]).then_inc(ysq_done, 1)
                act.wait_ge(yss_done, t + 1)
                nc.scalar.activation(ysd[:], yss[:], ACT.Sqrt, scale=1.0 / D, bias=eps[:]).then_inc(ysd_done, 1)

            with act.Fori(0, NT - 1) as t:
                with act.Fori(0, MH // 2) as hp:
                    for i in range(2):
                        head_step(t, hp, i)
                out_step(t, True)
            with act.Fori(0, MH // 2) as hp:
                for i in range(2):
                    head_step(NT - 1, hp, i)
            out_step(NT - 1, False)

        @block.vector
        def _(dve):
            def lo_of(m, slot):
                dve.wait_ge(w_hi_done, m + 1)
                nc.vector.tensor_tensor(w_lo[:, slot, :], w_raw[:, slot % RAW, :], w_hi[:, slot, :].bitcast(f32),
                                        ALU.subtract).then_inc(w_lo_done, 1)

            def rows_lo_of(r, s, hi, lo):
                dve.wait_ge(rows_hi, r + 1)
                nc.vector.tensor_tensor(lo, turned(s), hi.bitcast(f32), ALU.subtract).then_inc(rows_lo, 1)

            def norm_rows(s, rows, gain):
                nc.vector.scalar_tensor_tensor(out=rows, in0=rows, scalar=rs[:, s:s + 1], in1=gain,
                                               op0=ALU.mult, op1=ALU.mult).then_inc(rows_normed, 1)

            for credited in (z_done, b_used, gated, g_lo_done, y_final):
                dve.sem_inc(credited, CREDIT)
            dve.wait_ge(sd_done, 1)
            nc.vector.reciprocal(rs[:, 0:MT], sd[:, 0:MT]).then_inc(rs_done, 1)
            dve.wait_ge(gain_dma, 64)
            dve.wait_ge(rs_done, 1)
            for s in range(MT):
                norm_rows(s, x_res[:, s, :], mem_gain)
            for m in range(AHEAD):
                lo_of(m, m)
            for s in range(MT):
                rows_lo_of(s, s, g_hi[:, 0:KT, s * P:(s + 1) * P], g_lo[:, 0:KT, s * P:(s + 1) * P])
            dve.wait_ge(sd_done, 2)
            dve.wait_ge(rows_normed, MT)
            nc.vector.reciprocal(rs[:], sd[:]).then_inc(rs_done, 1)
            dve.wait_ge(rs_done, 2)
            for s in range(SUB):
                norm_rows(s, x_in[:, s, :], pre_gain[:])
            for s in range(SUB):
                rows_lo_of(MT + s, s, h_hi[:, :, s * P:(s + 1) * P], h_lo[:, :, s * P:(s + 1) * P])
            for m in range(NKV):
                lo_of(m + AHEAD, (m + AHEAD) % RING)
                if 1 <= m <= MH:
                    dve.wait_ge(kv_hi_done, m)
                    nc.vector.tensor_tensor(k_lo[:, m - 1, :], psum[:, m - 1, 0:NM], k_hi[:, m - 1, :].bitcast(f32),
                                            ALU.subtract).then_inc(kv_lo_done, 1)
            for m in range(MT):
                dve.wait_ge(kv_hi_done, MH + m + 1)
                nc.vector.tensor_tensor(v_lo[:, m, :], psum[:, m, :], v_hi[:, m, :].bitcast(f32),
                                        ALU.subtract).then_inc(kv_lo_done, 1)
            dve.wait_ge(kv_lo_done, MH + MT)

            def head_step(t, hp, i):
                h = t * MH + hp * 2 + i
                n = NKV + t * TILE_BLOCKS + hp * PAIR_BLOCKS + i * HEAD_BLOCKS

                def ahead(p):
                    a = i * HEAD_BLOCKS + p + AHEAD
                    lo_of(n + p + AHEAD, a % RING)

                def came(p):
                    dve.wait_ge(blocks_done, n + p + 1)

                def make_z(p, jj):
                    j = h * 2 + jj
                    own = hp * 4 + i * 2 + jj
                    halo = flat(z_halo[:, ds(own, 1), :])
                    dve.wait_ge(b_used, CREDIT + j)
                    nc.vector.tensor_scalar(z[:, 0:HALO], halo, 1.0, None, ALU.mult).then_inc(halo_in, 1)
                    came(p)
                    dve.wait_ge(c_done, j + 1)
                    nc.vector.tensor_tensor(z[:, HALO:], psum[:, 2, :], c_sb[:], ALU.mult).then_inc(z_done, 1)
                    dve.wait_ge(halo_in, j + 1)
                    dve.wait_ge(z_done, CREDIT + j + 1)
                    nc.vector.tensor_scalar(halo, z[:, TILE:TILE + HALO], 1.0, None, ALU.mult).then_inc(halo_out, 1)

                def convolve(p, jj):
                    j = h * 2 + jj
                    dve.wait_ge(halo_out, j + 1)
                    w = flat(conv_w[:, ds(hp * 4 + i * 2 + jj, 1), :])
                    dve.wait_ge(g_lo_done, CREDIT + h * 3 + jj)
                    nc.vector.tensor_scalar(mix[:], z[:, 2:2 + TILE], w[:, 2:3], None, ALU.mult).then_inc(tap2_done, 1)
                    dve.wait_ge(tap2_done, j + 1)
                    nc.vector.scalar_tensor_tensor(out=mix[:], in0=z[:, 1:1 + TILE], scalar=w[:, 1:2], in1=mix[:],
                                                   op0=ALU.mult, op1=ALU.add).then_inc(tap1_done, 1)
                    dve.wait_ge(tap1_done, j + 1)
                    nc.vector.scalar_tensor_tensor(out=mix[:], in0=z[:, 0:TILE], scalar=w[:, 0:1], in1=mix[:],
                                                   op0=ALU.mult, op1=ALU.add).then_inc(tap0_done, 1)
                    came(p)
                    dve.wait_ge(tap0_done, j + 1)
                    nc.vector.tensor_tensor(mix[:], psum[:, 3, :], mix[:], ALU.mult).then_inc(b_used, 1)

                def gate_it(item, silu_n, src, at):
                    dve.wait_ge(silu_done, silu_n)
                    nc.vector.tensor_tensor(mix[:], src, silu[:], ALU.mult).then_inc(gated, 1)
                    dve.wait_ge(g_hi_done, h * 3 + item + 1)
                    nc.vector.tensor_tensor(flat(g_lo[:, ds(at, 1), :]), mix[:],
                                            flat(g_hi[:, ds(at, 1), :]).bitcast(f32), ALU.subtract).then_inc(g_lo_done, 1)

                ahead(Q)
                dve.wait_ge(q_hi_done, h + 1)
                nc.vector.tensor_tensor(q_lo[:], psum[:, 0, :], q_hi[:].bitcast(f32), ALU.subtract).then_inc(q_lo_done, 1)
                ahead(C0)
                for src, dst in ((v_hi, vh_hi), (v_lo, vh_lo)):
                    nc.vector.tensor_scalar(dst[:], src[:, :, ds((hp * 2 + i) * HD, HD)].bitcast(f32), 1.0, None,
                                            ALU.mult).then_inc(vh_done, 1)
                ahead(U0)
                make_z(U0, 0)
                dve.wait_ge(scores_done, h + 1)
                nc.vector.tensor_reduce(rmax[:], scores, AX.X, ALU.max).then_inc(rmax_done, 1)
                dve.wait_ge(rmax_done, h + 1)
                nc.vector.tensor_scalar(nmax[:], rmax[:], -SCALE, None, ALU.mult).then_inc(nmax_done, 1)
                ahead(B0)
                convolve(B0, 0)
                dve.wait_ge(exp_done, (h + 1) * SUB)
                nc.vector.reciprocal(rinv[:], rsum[:]).then_inc(rinv_done, 1)
                dve.wait_ge(rinv_done, h + 1)
                for s in range(SUB):
                    nc.vector.tensor_scalar(probs[:, s, :], probs[:, s, :], rinv[:, s:s + 1], None,
                                            ALU.mult).then_inc(probs_done, 1)
                ahead(G0)
                dve.wait_ge(b_used, CREDIT + h * 2 + 1)
                gate_it(0, CREDIT + h * 3 + 1, mix[:], hp * 4 + i * 2)
                ahead(C1)
                dve.wait_ge(pt_hi_done, h + 1)
                nc.vector.tensor_tensor(flat(pt_lo[:]), flat(probs_t), flat(pt_hi[:]).bitcast(f32),
                                        ALU.subtract).then_inc(pt_lo_done, 1)
                ahead(U1)
                make_z(U1, 1)
                ahead(B1)
                convolve(B1, 1)
                ahead(G1)
                dve.wait_ge(b_used, CREDIT + h * 2 + 2)
                gate_it(1, CREDIT + h * 3 + 2, mix[:], hp * 4 + i * 2 + 1)
                ahead(MG)
                dve.wait_ge(pv_done, h + 1)
                dve.wait_ge(g_lo_done, CREDIT + h * 3 + 2)
                gate_it(2, CREDIT + h * 3 + 3, mem_o, hp * 2 + i + CH)

            def out_step(t, more):
                n = NKV + t * TILE_BLOCKS + IN_BLOCKS
                r = MT + (t + 1) * SUB
                for p in range(OUT_BLOCKS):
                    if more or p + AHEAD < OUT_BLOCKS:
                        lo_of(n + p + AHEAD, (p + AHEAD) % RING)
                    if more and p == 0:
                        dve.wait_ge(sd_done, t + 3)
                        nc.vector.reciprocal(rs[:], sd[:]).then_inc(rs_done, 1)
                        dve.wait_ge(rs_done, t + 3)
                    if more and p < 2:
                        for s in (2 * p, 2 * p + 1):
                            norm_rows(s, x_in[:, s, :], pre_gain[:])
                    if more and 2 <= p < 2 + SUB:
                        s = p - 2
                        rows_lo_of(r + s, s, h_hi[:, :, s * P:(s + 1) * P], h_lo[:, :, s * P:(s + 1) * P])
                dve.wait_ge(ysq_done, (t + 1) * 2 * SUB)
                nc.vector.tensor_tensor(yss[:], ysq[:, 0, :], ysq[:, 1, :], ALU.add).then_inc(yss_done, 1)
                dve.wait_ge(ysd_done, t + 1)
                nc.vector.reciprocal(yrs[:], ysd[:]).then_inc(yrs_done, 1)
                dve.wait_ge(yrs_done, t + 1)

                def scale_y(s):
                    for half, src in ((0, y_left[:, s, :]), (1, psum[:, 4 + s, :])):
                        nc.vector.scalar_tensor_tensor(
                            out=src, in0=src, scalar=yrs[:, s:s + 1], in1=post_gain[:, half * HALF:(half + 1) * HALF],
                            op0=ALU.mult, op1=ALU.mult).then_inc(y_scaled, 1)

                def add_x(s):
                    i = s % RES
                    before = 1 if i < MT else 0
                    dve.wait_ge(x_res_dma[i], (before + t * per_tile(i) + s // RES + 1) * 16)
                    for half, src in ((0, y_left[:, s, :]), (1, psum[:, 4 + s, :])):
                        dve.wait_ge(y_scaled, (t * SUB + s) * 2 + half + 1)
                        cols = x_res[:, i, half * HALF:(half + 1) * HALF]
                        op = nc.vector.tensor_tensor(cols, src, cols, ALU.add)
                    op.then_inc(y_final, 1)

                for s in range(SUB):
                    scale_y(s)
                    add_x(s)

            with dve.Fori(0, NT - 1) as t:
                with dve.Fori(0, MH // 2) as hp:
                    for i in range(2):
                        head_step(t, hp, i)
                out_step(t, True)
            with dve.Fori(0, MH // 2) as hp:
                for i in range(2):
                    head_step(NT - 1, hp, i)
            out_step(NT - 1, False)

        @block.tensor
        def _(pe):
            def product(dst, left, right, first, last):
                (a, b), (c, d) = left, right
                nc.tensor.matmul(dst, a, c, start=first, stop=False)
                nc.tensor.matmul(dst, a, d, start=False, stop=False)
                return nc.tensor.matmul(dst, b, c, start=False, stop=last)

            def turn_rows(s, rows):
                for k in range(KT):
                    op = nc.tensor.transpose(turned(s)[:, k, :], rows[:, k * P:(k + 1) * P], ident[:])
                op.then_inc(rows_turned, 1)

            pe.wait_ge(consts_set, 4)
            for s in range(MT):
                pe.wait_ge(rows_normed, s + 1)
                turn_rows(s, x_res[:, s, :])
            for s in range(SUB):
                pe.wait_ge(rows_normed, MT + s + 1)
                pe.wait_ge(rows_lo, s + 1)
                turn_rows(s, x_in[:, s, :])

            for m in range(MH):
                pe.wait_ge(w_lo_done, m + 1)
                for k in range(KT):
                    w = [a[:, m % RING, k * P:(k + 1) * P] for a in (w_hi, w_lo)]
                    op = product(psum[:, m, 0:NM], w, [a[:, k, 0:NM] for a in (g_hi, g_lo)], k == 0, k == KT - 1)
                op.then_inc(blocks_done, 1)
            for m in range(MH, NKV):
                pe.wait_ge(w_lo_done, m + 1)
                if m == MH:
                    pe.wait_ge(kv_lo_done, MT)
                for kk in range(2):
                    k = (m - MH) * 2 + kk
                    for a in range(MT):
                        rows = [u[:, k, a * P:(a + 1) * P] for u in (g_hi, g_lo)]
                        w = [u[:, m % RING, kk * HALF:(kk + 1) * HALF] for u in (w_hi, w_lo)]
                        op = product(psum[:, a, :], rows, w, k == 0, k == KT - 1)
                op.then_inc(blocks_done, 1)
            pe.wait_ge(kv_lo_done, MH + MT)
            pe.wait_ge(rows_lo, MT + SUB)

            def head_step(t, hp, i):
                h = t * MH + hp * 2 + i
                j = h * 2
                n = NKV + t * TILE_BLOCKS + hp * PAIR_BLOCKS + i * HEAD_BLOCKS

                def project(p, bank):
                    slot = (i * HEAD_BLOCKS + p) % RING
                    pe.wait_ge(w_lo_done, n + p + 1)
                    for k in range(KT):
                        w = [a[:, slot, k * P:(k + 1) * P] for a in (w_hi, w_lo)]
                        op = product(psum[:, bank, :], w, [a[:, k, :] for a in (h_hi, h_lo)], k == 0, k == KT - 1)
                    op.then_inc(blocks_done, 1)

                pe.wait_ge(silu_done, CREDIT + h * 3)
                project(Q, 0)
                project(C0, 1)
                pe.wait_ge(z_done, CREDIT + j)
                project(U0, 2)
                pe.wait_ge(q_lo_done, h + 1)
                pe.wait_ge(g_lo_done, CREDIT + h * 3)
                pe.wait_ge(y_final, CREDIT + t * SUB)
                head = hp * 2 + i
                keys = [flat(a[:, ds(head, 1), :]) for a in (k_hi, k_lo)]
                for s in range(SUB):
                    op = product(scores[:, s, :], [a[:, s * P:(s + 1) * P] for a in (q_hi, q_lo)], keys, True, True)
                op.then_inc(scores_done, 1)
                pe.wait_ge(b_used, CREDIT + j)
                project(B0, 3)
                project(G0, 0)
                pe.wait_ge(probs_done, (h + 1) * SUB)
                for s in range(SUB):
                    for a in range(MT):
                        op = nc.tensor.transpose(probs_t[:, a, s * P:(s + 1) * P], probs[:, s, a * P:(a + 1) * P], ident[:])
                op.then_inc(turned_done, 1)
                pe.wait_ge(c_done, j + 1)
                project(C1, 1)
                pe.wait_ge(z_done, CREDIT + j + 1)
                project(U1, 2)
                pe.wait_ge(pt_lo_done, h + 1)
                pe.wait_ge(vh_done, (h + 1) * 2)
                for a in range(MT):
                    op = product(mem_o, [u[:, a, :] for u in (vh_hi, vh_lo)], [u[:, a, :] for u in (pt_hi, pt_lo)],
                                 a == 0, a == MT - 1)
                op.then_inc(pv_done, 1)
                pe.wait_ge(b_used, CREDIT + j + 1)
                project(B1, 3)
                pe.wait_ge(silu_done, CREDIT + h * 3 + 1)
                project(G1, 0)
                pe.wait_ge(c_done, j + 2)
                project(MG, 1)

            def out_step(t, more):
                n = NKV + t * TILE_BLOCKS + IN_BLOCKS
                r = MT + (t + 1) * SUB
                pe.wait_ge(silu_done, CREDIT + (t + 1) * MH * 3)
                pe.wait_ge(b_used, CREDIT + (t + 1) * CH)
                for p in range(OUT_BLOCKS):
                    right, b = divmod(p, OUT_BLOCKS // 2)
                    pe.wait_ge(w_lo_done, n + p + 1)
                    if not right:
                        step = t * MH + (b if b < MH else MH - 1)
                        pe.wait_ge(g_lo_done, CREDIT + step * 3 + (2 if b < MH else 3))
                    for kk in range(2):
                        k = 2 * b + kk
                        for s in range(SUB):
                            g = [a[:, k, s * P:(s + 1) * P] for a in (g_hi, g_lo)]
                            w = [a[:, p % RING, kk * HALF:(kk + 1) * HALF] for a in (w_hi, w_lo)]
                            if p == OUT_BLOCKS // 2 and kk == 0 and more:
                                if s % 2 == 0:
                                    pe.wait_ge(rows_lo, r + 3 + s // 2)
                            op = product(psum[:, 4 * right + s, :], g, w, k == 0, k == BT - 1)
                            if right and k == BT - 1 and s < SUB - 1:
                                op.then_inc(y_right_done, 1)
                    op.then_inc(blocks_done, 1)
                    if more and 1 <= p <= SUB:
                        s = p - 1
                        pe.wait_ge(rows_normed, r + s + 1)
                        if s < 2:
                            pe.wait_ge(g_lo_done, CREDIT + (t + 1) * MH * 3)
                        else:
                            pe.wait_ge(rows_lo, r + s - 1)
                        turn_rows(s, x_in[:, s, :])
                pe.wait_ge(y_left_done, (t + 1) * SUB)
                pe.wait_ge(ysq_done, t * 2 * SUB + SUB)

            with pe.Fori(0, NT - 1) as t:
                with pe.Fori(0, MH // 2) as hp:
                    for i in range(2):
                        head_step(t, hp, i)
                out_step(t, True)
            with pe.Fori(0, MH // 2) as hp:
                for i in range(2):
                    head_step(NT - 1, hp, i)
            out_step(NT - 1, False)


def kernel(**inputs):
    import numpy as np
    import concourse.bacc as bacc
    from concourse.bass_utils import run_bass_kernel_spmd

    def proj_block(w, col):
        return w[:, col:col + P].reshape(KT, P, P).transpose(1, 0, 2).reshape(P, BLOCK)

    def wide_block(w, k, col):
        return w[k * P:(k + 2) * P, col:col + HALF].reshape(2, P, HALF).transpose(1, 0, 2).reshape(P, BLOCK)

    w_in = np.asarray(inputs["w_in_a"])[0]
    w_out = np.asarray(inputs["w_out"])[0]
    w_kv = np.asarray(inputs["w_mem_kv"])[0]
    b_col, c_col, u_col, gate_col, q_col = 0, D, 2 * D, 3 * D, 3 * D + BR
    order = [proj_block(w_kv, m * P) for m in range(MH)]
    order += [wide_block(w_kv, k, MH * HD) for k in range(0, KT, 2)]
    for h in range(MH):
        order.append(proj_block(w_in, q_col + h * P))
        for j in (2 * h, 2 * h + 1):
            order += [proj_block(w_in, col + j * P) for col in (c_col, u_col, b_col, gate_col)]
        order.append(proj_block(w_in, gate_col + D + h * P))
    for col in (0, HALF):
        order += [wide_block(w_out, k, col) for k in range(0, BT, 2)]

    def on_all(row):
        return np.repeat(np.asarray(row).reshape(1, D), P, axis=0)

    ins = {
        "x": np.asarray(inputs["x"])[0],
        "mem": np.asarray(inputs["mem"])[0],
        "pre_g": on_all(inputs["pre_norm"]),
        "post_g": on_all(inputs["post_norm"]),
        "mem_g": on_all(inputs["mem_norm"]),
        "conv": np.asarray(inputs["conv_a"])[0].reshape(CONV, CH, P).transpose(2, 1, 0),
        "blocks": np.stack(order),
    }
    nc = bacc.Bacc("TRN2", target_bir_lowering=False, num_devices=1)
    arrays, args = {}, []
    for name, a in ins.items():
        arrays[f"in_{name}"] = np.ascontiguousarray(a)
        args.append(nc.dram_tensor(f"in_{name}", list(a.shape), mybir.dt.from_np(a.dtype), kind="ExternalInput").ap())
    out = nc.dram_tensor("out_x", [SEQ, D], mybir.dt.float32, kind="ExternalOutput").ap()
    trunk(nc, *args, out)
    r = run_bass_kernel_spmd(nc, [arrays], core_ids=[0])
    return np.asarray(r.results[0]["out_x"]).reshape(1, SEQ, D)
```

```python
from contextlib import ExitStack

import concourse.bass as bass
from concourse import mybir

P = 128
D = 1024
SEQ = 4096
TILE = 512
NT = SEQ // TILE
SUB = TILE // P
KT = D // P
CH = D // P
CONV = 3
HALO = CONV - 1
MH = 4
HD = 128
NM = 256
MT = NM // P
BR = D + MH * HD
BT = BR // P
HALF = 512
PAIRS = KT // 2
MPAIRS = 2
BLOCK = 1024
NKV = 2 * MH * HD * D // (P * BLOCK)
HEAD_BLOCKS = 2 + 2 * 4
PAIR_BLOCKS = 2 * HEAD_BLOCKS
IN_BLOCKS = MH * HEAD_BLOCKS
OUT_BLOCKS = BT * D // BLOCK
TILE_BLOCKS = IN_BLOCKS + OUT_BLOCKS
AHEAD = 3
RAW = 2
RING = AHEAD + 1
RES = 3
EPS = 1e-6
SCALE = HD ** -0.5
CREDIT = 2
Q, C0, U0, B0, G0, C1, U1, B1, G1, MG = range(HEAD_BLOCKS)


def trunk(nc, x, x_t, mem, in_gains, post_g, conv, blocks, out):
    f32 = mybir.dt.float32
    f32r = mybir.dt.float32r
    bf16 = mybir.dt.bfloat16
    ALU = mybir.AluOpType
    ACT = mybir.ActivationFunctionType
    AX = mybir.AxisListType
    ds = bass.ds

    with ExitStack() as ctx:
        def sb(name, shape, dt=f32):
            return ctx.enter_context(nc.sbuf_tensor(name, [P] + list(shape), dt))

        def sem(name):
            return ctx.enter_context(nc.semaphore(name))

        w_raw = sb("w_raw", [RAW, BLOCK])
        w_hi = sb("w_hi", [RING, BLOCK], f32r)
        w_lo = sb("w_lo", [RING, BLOCK], f32r)
        h_hi = sb("h_hi", [KT, TILE], f32r)
        h_lo = sb("h_lo", [KT, TILE], f32r)
        g_hi = sb("g_hi", [BT, TILE], f32r)
        g_lo = sb("g_lo", [BT, TILE], f32r)
        k_hi = sb("k_hi", [MH, NM], f32r)
        k_lo = sb("k_lo", [MH, NM], f32r)
        v_hi = sb("v_hi", [MT, MH * HD], f32r)
        v_lo = sb("v_lo", [MT, MH * HD], f32r)
        vh_hi = sb("vh_hi", [MT, HD], f32r)
        vh_lo = sb("vh_lo", [MT, HD], f32r)
        q_hi = sb("q_hi", [TILE], f32r)
        q_lo = sb("q_lo", [TILE], f32r)
        pt_hi = sb("pt_hi", [MT, TILE], f32r)
        pt_lo = sb("pt_lo", [MT, TILE], f32r)
        x_in = sb("x_in", [KT, TILE])
        x_res = sb("x_res", [RES, D])
        mem_in = x_res[:, 0:2, :].rearrange("p a (k m) -> p (a k) m", m=NM)
        gains = sb("gains", [2, KT])
        post_gain = sb("post_gain", [D])
        y_left = sb("y_left", [SUB, HALF])
        probs = y_left[:, 0:2, :].rearrange("p a (b m) -> p (a b) m", b=2)
        squares = y_left[:].rearrange("p a b -> p (a b)")
        sq_sum = sb("sq_sum", [2 * TILE])
        rs_all = sb("rs_all", [TILE])
        ones = sb("ones", [P])
        conv_w = sb("conv_w", [CH, CONV])
        z_halo = sb("z_halo", [CH, HALO])
        z = sb("z", [HALO + TILE])
        c_sb = sb("c_sb", [TILE])
        mix = sb("mix", [TILE])
        silu = sb("silu", [TILE])
        junk = sb("junk", [HALF], bf16)
        ident = sb("ident", [P])
        eps = sb("eps", [1])
        ysq = sb("ysq", [2, SUB])
        yss = sb("yss", [SUB])
        ysd = sb("ysd", [SUB])
        yrs = sb("yrs", [SUB])
        rmax = sb("rmax", [SUB])
        nmax = sb("nmax", [SUB])
        rsum = sb("rsum", [SUB])
        rinv = sb("rinv", [SUB])

        psum = ctx.enter_context(nc.psum_tensor("banks", [P, 8, HALF], f32))
        scores = psum[:, 4:6, :].rearrange("p a (b m) -> p (a b) m", b=2)
        probs_t = psum[:, 6:8, :]
        mem_o = psum[:, 4, :]

        token_sums = psum[:, 5, :]

        w_in_dma = [sem(f"w_in_dma{i}") for i in range(RAW)]
        x_in_dma = sem("x_in_dma")
        x_res_dma = [sem(f"x_res_dma{i}") for i in range(RES)]
        out_dma = [sem(f"out_dma{i}") for i in range(RES)]
        mem_dma = sem("mem_dma")
        gains_dma = sem("gains_dma")
        post_dma = sem("post_dma")
        consts_set = sem("consts_set")
        pool_passed = sem("pool_passed")
        w_hi_done = sem("w_hi_done")
        w_lo_done = sem("w_lo_done")
        blocks_done = sem("blocks_done")
        sq_done = sem("sq_done")
        sq_added = sem("sq_added")
        sums_done = sem("sums_done")
        sd_done = sem("sd_done")
        rs_done = sem("rs_done")
        normed = sem("normed")
        h_hi_done = sem("h_hi_done")
        h_lo_done = sem("h_lo_done")
        kv_hi_done = sem("kv_hi_done")
        kv_lo_done = sem("kv_lo_done")
        vh_done = sem("vh_done")
        q_hi_done = sem("q_hi_done")
        q_lo_done = sem("q_lo_done")
        scores_done = sem("scores_done")
        rmax_done = sem("rmax_done")
        nmax_done = sem("nmax_done")
        exp_done = sem("exp_done")
        rinv_done = sem("rinv_done")
        probs_done = sem("probs_done")
        turned_done = sem("turned_done")
        pt_hi_done = sem("pt_hi_done")
        pt_lo_done = sem("pt_lo_done")
        pv_done = sem("pv_done")
        c_done = sem("c_done")
        halo_in = sem("halo_in")
        z_done = sem("z_done")
        halo_out = sem("halo_out")
        tap2_done = sem("tap2_done")
        tap1_done = sem("tap1_done")
        tap0_done = sem("tap0_done")
        b_used = sem("b_used")
        silu_done = sem("silu_done")
        gated = sem("gated")
        g_hi_done = sem("g_hi_done")
        g_lo_done = sem("g_lo_done")
        y_left_done = sem("y_left_done")
        y_right_done = sem("y_right_done")
        ysq_done = sem("ysq_done")
        yss_done = sem("yss_done")
        ysd_done = sem("ysd_done")
        yrs_done = sem("yrs_done")
        y_scaled = sem("y_scaled")
        y_final = sem("y_final")

        block = ctx.enter_context(nc.Block())

        def per_tile(i):
            return len(range(i, SUB, RES))

        def flat(ap):
            return ap.rearrange("p a b -> p (a b)")

        @block.sync
        def _(sp):
            def load(m, slot, src):
                sp.dma_start(w_raw[:, slot, :], src).then_inc(w_in_dma[slot], 16)

            sp.dma_start(mem_in, mem).then_inc(mem_dma, 16)
            for m in range(NKV):
                if m >= RAW:
                    sp.wait_ge(w_lo_done, m - RAW + 1)
                load(m, m % RAW, blocks[m])
            with sp.Fori(0, NT) as t:
                with sp.Fori(0, TILE_BLOCKS // RAW) as pair:
                    for i in range(RAW):
                        m = NKV + t * TILE_BLOCKS + pair * RAW + i
                        sp.wait_ge(w_lo_done, m - RAW + 1)
                        src = blocks[ds(NKV + pair * RAW + i, 1), :, :].rearrange("a p n -> p (a n)")
                        load(m, i, src)

        @block.gpsimd
        def _(pool):
            pool.dma_start(gains[:], in_gains).then_inc(gains_dma, 16)
            pool.dma_start(x_in[:], x_t[0]).then_inc(x_in_dma, 16)
            pool.dma_start(conv_w[:], conv).then_inc(post_dma, 16)
            pool.dma_start(post_gain[:], post_g).then_inc(post_dma, 16)
            pool.memset(ones[:], 1.0).then_inc(consts_set, 1)
            pool.memset(eps[:], EPS).then_inc(consts_set, 1)
            pool.memset(z_halo[:], 0.0).then_inc(consts_set, 1)
            pool.memset(ident[:], 0.0).then_inc(consts_set, 1)
            pool.wait_ge(consts_set, 4)
            pool.affine_select(out=ident[:], in_=ident[:], compare_op=ALU.not_equal, fill=1.0, base=0,
                               pattern=[[-1, P]], channel_multiplier=1).then_inc(consts_set, 1)

            def load_residual(t, s):
                pool.dma_start(x_res[:, s % RES, :], x[ds((t * SUB + s) * P, P), :]).then_inc(x_res_dma[s % RES], 16)

            def tile(t, more):
                for s in range(RES):
                    load_residual(t, s)
                if more:
                    pool.wait_ge(h_lo_done, MPAIRS + (t + 1) * PAIRS)
                    pool.sem_inc(pool_passed, 1)
                    pool.dma_start(x_in[:], x_t[ds(t + 1, 1)].rearrange("a p k n -> p (a k) n")).then_inc(x_in_dma, 16)
                for s in range(SUB):
                    pool.wait_ge(y_final, CREDIT + t * SUB + s + 1)
                    pool.sem_inc(pool_passed, 1)
                    pool.dma_start(out[ds((t * SUB + s) * P, P), :], x_res[:, s % RES, :]).then_inc(out_dma[s % RES], 16)
                    if s + RES < SUB:
                        pool.wait_ge(out_dma[s], (t * 2 + 1) * 16)
                        pool.sem_inc(pool_passed, 1)
                        load_residual(t, s + RES)
                for i in range(RES):
                    pool.wait_ge(out_dma[i], (t + 1) * per_tile(i) * 16)

            pool.wait_ge(h_lo_done, MPAIRS)
            with pool.Fori(0, NT - 1) as t:
                tile(t, True)
            tile(NT - 1, False)

        @block.scalar
        def _(act):
            def hi_of(m_half, m, slot):
                act.wait_ge(w_in_dma[slot % RAW], (m_half + 1) * 16)
                act.wait_ge(blocks_done, m - RING + 1)
                nc.scalar.activation(w_hi[:, slot, :], w_raw[:, slot % RAW, :], ACT.Copy).then_inc(w_hi_done, 1)

            def square(which, src):
                act.wait_ge(sq_added, which)
                nc.scalar.activation(squares, flat(src), ACT.Square).then_inc(sq_done, 1)

            def root(nth, dst, src):
                act.wait_ge(sums_done, nth)
                nc.scalar.activation(dst, src, ACT.Sqrt, scale=1.0 / D, bias=eps[:]).then_inc(sd_done, 1)

            def hi_of_pair(tile, a):
                act.wait_ge(normed, (tile + 1) * KT + 2 * a + 2)
                nc.scalar.activation(h_hi[:, 2 * a:2 * a + 2, :], x_in[:, 2 * a:2 * a + 2, :], ACT.Copy).then_inc(h_hi_done, 1)

            def first_hi(m):
                act.wait_ge(w_in_dma[m % RAW], (m // RAW + 1) * 16)
                if m >= RING:
                    act.wait_ge(blocks_done, m - RING + 1)
                nc.scalar.activation(w_hi[:, m % RING, :], w_raw[:, m % RAW, :], ACT.Copy).then_inc(w_hi_done, 1)

            act.sem_inc(silu_done, CREDIT)
            act.wait_ge(mem_dma, 16)
            nc.scalar.activation(squares, flat(mem_in), ACT.Square).then_inc(sq_done, 1)
            act.wait_ge(consts_set, 5)
            root(1, rs_all[:, 0:NM], token_sums[:, 0:NM])
            for m in range(AHEAD):
                first_hi(m)
            for a in range(MPAIRS):
                ks = slice(a * KT // 2, (a + 1) * KT // 2)
                act.wait_ge(normed, (a + 1) * KT // 2)
                nc.scalar.activation(g_hi[:, ks, 0:NM], mem_in[:, ks, :], ACT.Copy).then_inc(h_hi_done, 1)
            act.wait_ge(x_in_dma, 16)
            square(3, x_in[:, 0:KT // 2, :])
            square(4, x_in[:, KT // 2:, :])
            for m in range(NKV):
                first_hi(m + AHEAD)
                if 1 <= m <= MH:
                    act.wait_ge(blocks_done, m)
                    nc.scalar.activation(k_hi[:, m - 1, :], psum[:, m - 1, 0:NM], ACT.Copy).then_inc(kv_hi_done, 1)
                if m == MH - 1:
                    root(2, rs_all[:], token_sums)
                if m >= MH:
                    hi_of_pair(0, m - MH)
            act.wait_ge(blocks_done, NKV)
            for m in range(MT):
                nc.scalar.activation(v_hi[:, m, :], psum[:, m, :], ACT.Copy).then_inc(kv_hi_done, 1)

            def head_step(t, hp, i):
                h = t * MH + hp * 2 + i
                j = h * 2
                n = NKV + t * TILE_BLOCKS + hp * PAIR_BLOCKS + i * HEAD_BLOCKS
                half = NKV // 2 + t * (TILE_BLOCKS // 2) + hp * (PAIR_BLOCKS // 2) + i * (HEAD_BLOCKS // 2)

                def ahead(p):
                    a = i * HEAD_BLOCKS + p + AHEAD
                    hi_of(half + (p + AHEAD) // 2, n + p + AHEAD, a % RING)

                def came(p):
                    act.wait_ge(blocks_done, n + p + 1)

                def gate(p, bank, item):
                    came(p)
                    act.wait_ge(gated, CREDIT + h * 3 + item)
                    nc.scalar.activation(silu[:], psum[:, bank, :], ACT.Silu).then_inc(silu_done, 1)

                def hi_of_gated(item, dst):
                    act.wait_ge(gated, CREDIT + h * 3 + item + 1)
                    nc.scalar.activation(dst, mix[:], ACT.Copy).then_inc(g_hi_done, 1)

                ahead(Q)
                came(Q)
                nc.scalar.activation(q_hi[:], psum[:, 0, :], ACT.Copy).then_inc(q_hi_done, 1)
                ahead(C0)
                came(C0)
                act.wait_ge(z_done, CREDIT + j)
                nc.scalar.activation(c_sb[:], psum[:, 1, :], ACT.Copy).then_inc(c_done, 1)
                ahead(U0)
                ahead(B0)
                ahead(G0)
                act.wait_ge(nmax_done, h + 1)
                if i == 0:
                    act.wait_ge(y_final, CREDIT + t * SUB)
                for s in range(SUB):
                    op = nc.scalar.activation(probs[:, s, :], scores[:, s, :], ACT.Exp, scale=SCALE,
                                              bias=nmax[:, s:s + 1], accum_out=rsum[:, s:s + 1])
                    op.then_inc(exp_done, 1)
                gate(G0, 0, 0)
                ahead(C1)
                hi_of_gated(0, flat(g_hi[:, ds(hp * 4 + i * 2, 1), :]))
                came(C1)
                act.wait_ge(z_done, CREDIT + j + 1)
                nc.scalar.activation(c_sb[:], psum[:, 1, :], ACT.Copy).then_inc(c_done, 1)
                ahead(U1)
                ahead(B1)
                act.wait_ge(turned_done, h + 1)
                nc.scalar.activation(flat(pt_hi[:]), flat(probs_t), ACT.Copy).then_inc(pt_hi_done, 1)
                ahead(G1)
                gate(G1, 0, 1)
                ahead(MG)
                hi_of_gated(1, flat(g_hi[:, ds(hp * 4 + i * 2 + 1, 1), :]))
                gate(MG, 3, 2)
                hi_of_gated(2, flat(g_hi[:, ds(hp * 2 + i + CH, 1), :]))

            def out_step(t, more):
                n = NKV + t * TILE_BLOCKS + IN_BLOCKS
                half = NKV // 2 + t * (TILE_BLOCKS // 2) + IN_BLOCKS // 2
                nth = t + 1
                for p in range(OUT_BLOCKS):
                    if more or p + AHEAD < OUT_BLOCKS:
                        hi_of(half + (p + AHEAD) // 2, n + p + AHEAD, (p + AHEAD) % RING)
                    if more and p == 0:
                        act.wait_ge(x_in_dma, (nth + 1) * 16)
                        act.wait_ge(turned_done, (t + 1) * MH)
                        square(3 + nth * 4, x_in[:, 0:KT // 2, :])
                    if more and p == 1:
                        square(4 + nth * 4, x_in[:, KT // 2:, :])
                    if more and p == 4:
                        root(nth + 2, rs_all[:], token_sums)
                    if more and 5 <= p < 5 + PAIRS:
                        hi_of_pair(nth, p - 5)
                    if p == OUT_BLOCKS // 2:
                        act.wait_ge(blocks_done, n + p)
                        for s in range(SUB):
                            if s:
                                act.wait_ge(ysq_done, t * 2 * SUB + s)
                            nc.scalar.activation(junk[:], psum[:, s, :], ACT.Square,
                                                 accum_out=ysq[:, 0, s:s + 1]).then_inc(ysq_done, 1)
                for s in range(SUB):
                    if s < SUB - 1:
                        act.wait_ge(y_right_done, t * (SUB - 1) + s + 1)
                    else:
                        act.wait_ge(blocks_done, n + OUT_BLOCKS)
                    act.wait_ge(ysq_done, t * 2 * SUB + SUB + s)
                    nc.scalar.activation(junk[:], psum[:, 4 + s, :], ACT.Square,
                                         accum_out=ysq[:, 1, s:s + 1]).then_inc(ysq_done, 1)
                act.wait_ge(yss_done, t + 1)
                nc.scalar.activation(ysd[:], yss[:], ACT.Sqrt, scale=1.0 / D, bias=eps[:]).then_inc(ysd_done, 1)

            with act.Fori(0, NT - 1) as t:
                with act.Fori(0, MH // 2) as hp:
                    for i in range(2):
                        head_step(t, hp, i)
                out_step(t, True)
            with act.Fori(0, MH // 2) as hp:
                for i in range(2):
                    head_step(NT - 1, hp, i)
            out_step(NT - 1, False)

        @block.vector
        def _(dve):
            def lo_of(m, slot):
                dve.wait_ge(w_hi_done, m + 1)
                nc.vector.tensor_tensor(w_lo[:, slot, :], w_raw[:, slot % RAW, :], w_hi[:, slot, :].bitcast(f32),
                                        ALU.subtract).then_inc(w_lo_done, 1)

            def inverse(nth, n):
                dve.wait_ge(sd_done, nth)
                nc.vector.reciprocal(rs_all[:, 0:n], rs_all[:, 0:n]).then_inc(rs_done, 1)
                dve.wait_ge(rs_done, nth)

            def norm(rows, k, which, n):
                nc.vector.scalar_tensor_tensor(out=rows[:, k, :], in0=rows[:, k, :], scalar=gains[:, which, k:k + 1],
                                               in1=rs_all[:, 0:n], op0=ALU.mult, op1=ALU.mult).then_inc(normed, 1)

            def lo_of_pair(tile, a):
                dve.wait_ge(h_hi_done, MPAIRS + tile * PAIRS + a + 1)
                ks = slice(2 * a, 2 * a + 2)
                nc.vector.tensor_tensor(h_lo[:, ks, :], x_in[:, ks, :], h_hi[:, ks, :].bitcast(f32),
                                        ALU.subtract).then_inc(h_lo_done, 1)

            def add_squares(tile, half):
                before = 3 + tile * 4
                dve.wait_ge(sq_done, 1 + tile * 2 + half + 1)
                if not half:
                    dve.wait_ge(sq_added, before)
                    nc.vector.tensor_tensor(sq_sum[:], squares[:, 0:2 * TILE], squares[:, 2 * TILE:], ALU.add).then_inc(sq_added, 1)
                    return
                for i in range(2):
                    dve.wait_ge(sq_added, before + 1 + i)
                    nc.vector.tensor_tensor(sq_sum[:], squares[:, i * 2 * TILE:(i + 1) * 2 * TILE], sq_sum[:],
                                            ALU.add).then_inc(sq_added, 1)
                dve.wait_ge(sq_added, before + 3)
                nc.vector.tensor_tensor(sq_sum[:, 0:TILE], sq_sum[:, 0:TILE], sq_sum[:, TILE:], ALU.add).then_inc(sq_added, 1)

            for credited in (z_done, b_used, gated, g_lo_done, y_final):
                dve.sem_inc(credited, CREDIT)
            dve.wait_ge(sq_done, 1)
            nc.vector.tensor_tensor(sq_sum[:], squares[:, 0:4 * NM], squares[:, 4 * NM:], ALU.add).then_inc(sq_added, 1)
            for i, n in ((1, 2 * NM), (2, NM)):
                dve.wait_ge(sq_added, i)
                nc.vector.tensor_tensor(sq_sum[:, 0:n], sq_sum[:, 0:n], sq_sum[:, n:2 * n], ALU.add).then_inc(sq_added, 1)
            dve.wait_ge(gains_dma, 16)
            inverse(1, NM)
            for k in range(KT):
                norm(mem_in, k, 1, NM)
            for m in range(AHEAD):
                lo_of(m, m)
            for a in range(MPAIRS):
                ks = slice(a * KT // 2, (a + 1) * KT // 2)
                dve.wait_ge(h_hi_done, a + 1)
                nc.vector.tensor_tensor(g_lo[:, ks, 0:NM], mem_in[:, ks, :], g_hi[:, ks, 0:NM].bitcast(f32),
                                        ALU.subtract).then_inc(h_lo_done, 1)
            add_squares(0, 0)
            add_squares(0, 1)
            for m in range(NKV):
                lo_of(m + AHEAD, (m + AHEAD) % RING)
                if 1 <= m <= MH:
                    dve.wait_ge(kv_hi_done, m)
                    nc.vector.tensor_tensor(k_lo[:, m - 1, :], psum[:, m - 1, 0:NM], k_hi[:, m - 1, :].bitcast(f32),
                                            ALU.subtract).then_inc(kv_lo_done, 1)
                if m == MH - 1:
                    inverse(2, TILE)
                if m >= MH:
                    for k in (2 * (m - MH), 2 * (m - MH) + 1):
                        norm(x_in, k, 0, TILE)
                    lo_of_pair(0, m - MH)
            for m in range(MT):
                dve.wait_ge(kv_hi_done, MH + m + 1)
                nc.vector.tensor_tensor(v_lo[:, m, :], psum[:, m, :], v_hi[:, m, :].bitcast(f32),
                                        ALU.subtract).then_inc(kv_lo_done, 1)
            dve.wait_ge(kv_lo_done, MH + MT)
            dve.wait_ge(post_dma, 32)

            def head_step(t, hp, i):
                h = t * MH + hp * 2 + i
                n = NKV + t * TILE_BLOCKS + hp * PAIR_BLOCKS + i * HEAD_BLOCKS

                def ahead(p):
                    a = i * HEAD_BLOCKS + p + AHEAD
                    lo_of(n + p + AHEAD, a % RING)

                def came(p):
                    dve.wait_ge(blocks_done, n + p + 1)

                def make_z(p, jj):
                    j = h * 2 + jj
                    own = hp * 4 + i * 2 + jj
                    halo = flat(z_halo[:, ds(own, 1), :])
                    dve.wait_ge(b_used, CREDIT + j)
                    nc.vector.tensor_scalar(z[:, 0:HALO], halo, 1.0, None, ALU.mult).then_inc(halo_in, 1)
                    came(p)
                    dve.wait_ge(c_done, j + 1)
                    nc.vector.tensor_tensor(z[:, HALO:], psum[:, 2, :], c_sb[:], ALU.mult).then_inc(z_done, 1)
                    dve.wait_ge(halo_in, j + 1)
                    dve.wait_ge(z_done, CREDIT + j + 1)
                    nc.vector.tensor_scalar(halo, z[:, TILE:TILE + HALO], 1.0, None, ALU.mult).then_inc(halo_out, 1)

                def convolve(p, jj):
                    j = h * 2 + jj
                    dve.wait_ge(halo_out, j + 1)
                    w = flat(conv_w[:, ds(hp * 4 + i * 2 + jj, 1), :])
                    dve.wait_ge(g_lo_done, CREDIT + h * 3 + jj)
                    nc.vector.tensor_scalar(mix[:], z[:, 2:2 + TILE], w[:, 2:3], None, ALU.mult).then_inc(tap2_done, 1)
                    dve.wait_ge(tap2_done, j + 1)
                    nc.vector.scalar_tensor_tensor(out=mix[:], in0=z[:, 1:1 + TILE], scalar=w[:, 1:2], in1=mix[:],
                                                   op0=ALU.mult, op1=ALU.add).then_inc(tap1_done, 1)
                    dve.wait_ge(tap1_done, j + 1)
                    nc.vector.scalar_tensor_tensor(out=mix[:], in0=z[:, 0:TILE], scalar=w[:, 0:1], in1=mix[:],
                                                   op0=ALU.mult, op1=ALU.add).then_inc(tap0_done, 1)
                    came(p)
                    dve.wait_ge(tap0_done, j + 1)
                    nc.vector.tensor_tensor(mix[:], psum[:, 3, :], mix[:], ALU.mult).then_inc(b_used, 1)

                def gate_it(item, silu_n, src, at):
                    dve.wait_ge(silu_done, silu_n)
                    nc.vector.tensor_tensor(mix[:], src, silu[:], ALU.mult).then_inc(gated, 1)
                    dve.wait_ge(g_hi_done, h * 3 + item + 1)
                    nc.vector.tensor_tensor(flat(g_lo[:, ds(at, 1), :]), mix[:],
                                            flat(g_hi[:, ds(at, 1), :]).bitcast(f32), ALU.subtract).then_inc(g_lo_done, 1)

                ahead(Q)
                dve.wait_ge(q_hi_done, h + 1)
                nc.vector.tensor_tensor(q_lo[:], psum[:, 0, :], q_hi[:].bitcast(f32), ALU.subtract).then_inc(q_lo_done, 1)
                ahead(C0)
                for src, dst in ((v_hi, vh_hi), (v_lo, vh_lo)):
                    nc.vector.tensor_scalar(dst[:], src[:, :, ds((hp * 2 + i) * HD, HD)].bitcast(f32), 1.0, None,
                                            ALU.mult).then_inc(vh_done, 1)
                ahead(U0)
                make_z(U0, 0)
                ahead(B0)
                dve.wait_ge(scores_done, h + 1)
                nc.vector.tensor_reduce(rmax[:], scores, AX.X, ALU.max).then_inc(rmax_done, 1)
                dve.wait_ge(rmax_done, h + 1)
                nc.vector.tensor_scalar(nmax[:], rmax[:], -SCALE, None, ALU.mult).then_inc(nmax_done, 1)
                ahead(G0)
                convolve(B0, 0)
                dve.wait_ge(exp_done, (h + 1) * SUB)
                nc.vector.reciprocal(rinv[:], rsum[:]).then_inc(rinv_done, 1)
                dve.wait_ge(rinv_done, h + 1)
                for s in range(SUB):
                    nc.vector.tensor_scalar(probs[:, s, :], probs[:, s, :], rinv[:, s:s + 1], None,
                                            ALU.mult).then_inc(probs_done, 1)
                ahead(C1)
                dve.wait_ge(b_used, CREDIT + h * 2 + 1)
                gate_it(0, CREDIT + h * 3 + 1, mix[:], hp * 4 + i * 2)
                ahead(U1)
                make_z(U1, 1)
                ahead(B1)
                dve.wait_ge(pt_hi_done, h + 1)
                nc.vector.tensor_tensor(flat(pt_lo[:]), flat(probs_t), flat(pt_hi[:]).bitcast(f32),
                                        ALU.subtract).then_inc(pt_lo_done, 1)
                convolve(B1, 1)
                ahead(G1)
                dve.wait_ge(b_used, CREDIT + h * 2 + 2)
                gate_it(1, CREDIT + h * 3 + 2, mix[:], hp * 4 + i * 2 + 1)
                ahead(MG)
                dve.wait_ge(pv_done, h + 1)
                dve.wait_ge(g_lo_done, CREDIT + h * 3 + 2)
                gate_it(2, CREDIT + h * 3 + 3, mem_o, hp * 2 + i + CH)

            def out_step(t, more):
                n = NKV + t * TILE_BLOCKS + IN_BLOCKS
                nth = t + 1
                for p in range(OUT_BLOCKS):
                    if more or p + AHEAD < OUT_BLOCKS:
                        lo_of(n + p + AHEAD, (p + AHEAD) % RING)
                    if more and p < 2:
                        add_squares(nth, p)
                    if more and p == 4:
                        inverse(nth + 2, TILE)
                    if more and 5 <= p < 5 + PAIRS:
                        for k in (2 * (p - 5), 2 * (p - 5) + 1):
                            norm(x_in, k, 0, TILE)
                        lo_of_pair(nth, p - 5)
                    if p == OUT_BLOCKS // 2:
                        for s in range(SUB):
                            dve.wait_ge(ysq_done, t * 2 * SUB + s + 1)
                            nc.vector.tensor_tensor(y_left[:, s, :], psum[:, s, :], post_gain[:, 0:HALF],
                                                    ALU.mult).then_inc(y_left_done, 1)
                dve.wait_ge(ysq_done, (t + 1) * 2 * SUB)
                nc.vector.tensor_tensor(yss[:], ysq[:, 0, :], ysq[:, 1, :], ALU.add).then_inc(yss_done, 1)
                dve.wait_ge(ysd_done, t + 1)
                nc.vector.reciprocal(yrs[:], ysd[:]).then_inc(yrs_done, 1)
                dve.wait_ge(yrs_done, t + 1)

                for s in range(SUB):
                    i = s % RES
                    left, right = x_res[:, i, 0:HALF], x_res[:, i, HALF:]
                    y_right = psum[:, 4 + s, :]
                    nc.vector.scalar_tensor_tensor(out=y_right, in0=y_right, scalar=yrs[:, s:s + 1],
                                                   in1=post_gain[:, HALF:], op0=ALU.mult, op1=ALU.mult).then_inc(y_scaled, 1)
                    dve.wait_ge(x_res_dma[i], (t * per_tile(i) + s // RES + 1) * 16)
                    dve.wait_ge(y_left_done, t * SUB + s + 1)
                    nc.vector.scalar_tensor_tensor(out=left, in0=y_left[:, s, :], scalar=yrs[:, s:s + 1], in1=left,
                                                   op0=ALU.mult, op1=ALU.add)
                    dve.wait_ge(y_scaled, t * SUB + s + 1)
                    nc.vector.tensor_tensor(right, y_right, right, ALU.add).then_inc(y_final, 1)

            with dve.Fori(0, NT - 1) as t:
                with dve.Fori(0, MH // 2) as hp:
                    for i in range(2):
                        head_step(t, hp, i)
                out_step(t, True)
            with dve.Fori(0, MH // 2) as hp:
                for i in range(2):
                    head_step(NT - 1, hp, i)
            out_step(NT - 1, False)

        @block.tensor
        def _(pe):
            def product(dst, left, right, first, last):
                (a, b), (c, d) = left, right
                nc.tensor.matmul(dst, a, c, start=first, stop=False)
                nc.tensor.matmul(dst, a, d, start=False, stop=False)
                return nc.tensor.matmul(dst, b, c, start=False, stop=last)

            def sum_tokens(n, count):
                pe.wait_ge(sq_added, count)
                nc.tensor.matmul(token_sums[:, 0:n], ones[:], sq_sum[:, 0:n], start=True, stop=True).then_inc(sums_done, 1)

            pe.wait_ge(consts_set, 5)
            sum_tokens(NM, 3)
            pe.wait_ge(h_lo_done, MPAIRS)

            for m in range(MH):
                pe.wait_ge(w_lo_done, m + 1)
                for k in range(KT):
                    w = [a[:, m % RING, k * P:(k + 1) * P] for a in (w_hi, w_lo)]
                    op = product(psum[:, m, 0:NM], w, [a[:, k, 0:NM] for a in (g_hi, g_lo)], k == 0, k == KT - 1)
                op.then_inc(blocks_done, 1)
            sum_tokens(TILE, 3 + 4)
            for m in range(MH, NKV):
                pe.wait_ge(w_lo_done, m + 1)
                if m == MH:
                    pe.wait_ge(kv_lo_done, MT)
                for kk in range(2):
                    k = (m - MH) * 2 + kk
                    for a in range(MT):
                        rows = [u[:, k, a * P:(a + 1) * P] for u in (g_hi, g_lo)]
                        w = [u[:, m % RING, kk * HALF:(kk + 1) * HALF] for u in (w_hi, w_lo)]
                        op = product(psum[:, a, :], rows, w, k == 0, k == KT - 1)
                op.then_inc(blocks_done, 1)
            pe.wait_ge(kv_lo_done, MH + MT)
            pe.wait_ge(h_lo_done, MPAIRS + PAIRS)

            def head_step(t, hp, i):
                h = t * MH + hp * 2 + i
                j = h * 2
                n = NKV + t * TILE_BLOCKS + hp * PAIR_BLOCKS + i * HEAD_BLOCKS

                def project(p, bank):
                    slot = (i * HEAD_BLOCKS + p) % RING
                    pe.wait_ge(w_lo_done, n + p + 1)
                    for k in range(KT):
                        w = [a[:, slot, k * P:(k + 1) * P] for a in (w_hi, w_lo)]
                        op = product(psum[:, bank, :], w, [a[:, k, :] for a in (h_hi, h_lo)], k == 0, k == KT - 1)
                    op.then_inc(blocks_done, 1)

                pe.wait_ge(silu_done, CREDIT + h * 3 - 1)
                project(Q, 0)
                project(C0, 1)
                pe.wait_ge(z_done, CREDIT + j)
                project(U0, 2)
                pe.wait_ge(silu_done, CREDIT + h * 3)
                project(B0, 3)
                pe.wait_ge(q_lo_done, h + 1)
                pe.wait_ge(g_lo_done, CREDIT + h * 3)
                pe.wait_ge(y_final, CREDIT + t * SUB)
                head = hp * 2 + i
                keys = [flat(a[:, ds(head, 1), :]) for a in (k_hi, k_lo)]
                for s in range(SUB):
                    op = product(scores[:, s, :], [a[:, s * P:(s + 1) * P] for a in (q_hi, q_lo)], keys, True, True)
                op.then_inc(scores_done, 1)
                project(G0, 0)
                pe.wait_ge(c_done, j + 1)
                project(C1, 1)
                pe.wait_ge(z_done, CREDIT + j + 1)
                project(U1, 2)
                pe.wait_ge(probs_done, (h + 1) * SUB)
                for s in range(SUB):
                    for a in range(MT):
                        op = nc.tensor.transpose(probs_t[:, a, s * P:(s + 1) * P], probs[:, s, a * P:(a + 1) * P], ident[:])
                op.then_inc(turned_done, 1)
                pe.wait_ge(b_used, CREDIT + j + 1)
                project(B1, 3)
                pe.wait_ge(silu_done, CREDIT + h * 3 + 1)
                project(G1, 0)
                pe.wait_ge(pt_lo_done, h + 1)
                pe.wait_ge(vh_done, (h + 1) * 2)
                for a in range(MT):
                    op = product(mem_o, [u[:, a, :] for u in (vh_hi, vh_lo)], [u[:, a, :] for u in (pt_hi, pt_lo)],
                                 a == 0, a == MT - 1)
                op.then_inc(pv_done, 1)
                pe.wait_ge(b_used, CREDIT + j + 2)
                project(MG, 3)

            def out_step(t, more):
                n = NKV + t * TILE_BLOCKS + IN_BLOCKS
                nth = t + 1
                pe.wait_ge(silu_done, CREDIT + (t + 1) * MH * 3 - 1)
                pe.wait_ge(z_done, CREDIT + (t + 1) * CH)
                for p in range(OUT_BLOCKS):
                    right, b = divmod(p, OUT_BLOCKS // 2)
                    pe.wait_ge(w_lo_done, n + p + 1)
                    if not right:
                        step = t * MH + (b if b < MH else MH - 1)
                        pe.wait_ge(g_lo_done, CREDIT + step * 3 + (2 if b < MH else 3))
                    for kk in range(2):
                        k = 2 * b + kk
                        for s in range(SUB):
                            g = [a[:, k, s * P:(s + 1) * P] for a in (g_hi, g_lo)]
                            w = [a[:, p % RING, kk * HALF:(kk + 1) * HALF] for a in (w_hi, w_lo)]
                            if k == 0 and not right and s == SUB - 1:
                                pe.wait_ge(silu_done, CREDIT + (t + 1) * MH * 3)
                            if k == 0 and right and s == 1 and more:
                                pe.wait_ge(sd_done, nth + 2)
                            op = product(psum[:, 4 * right + s, :], g, w, k == 0, k == BT - 1)
                            if right and k == BT - 1 and s < SUB - 1:
                                op.then_inc(y_right_done, 1)
                    op.then_inc(blocks_done, 1)
                    if more and p == 3:
                        sum_tokens(TILE, 3 + (nth + 1) * 4)
                pe.wait_ge(y_left_done, (t + 1) * SUB)
                pe.wait_ge(ysq_done, t * 2 * SUB + SUB)
                if more:
                    pe.wait_ge(h_lo_done, MPAIRS + (nth + 1) * PAIRS)

            with pe.Fori(0, NT - 1) as t:
                with pe.Fori(0, MH // 2) as hp:
                    for i in range(2):
                        head_step(t, hp, i)
                out_step(t, True)
            with pe.Fori(0, MH // 2) as hp:
                for i in range(2):
                    head_step(NT - 1, hp, i)
            out_step(NT - 1, False)


def kernel(**inputs):
    import numpy as np
    import concourse.bacc as bacc
    from concourse.bass_utils import run_bass_kernel_spmd

    def proj_block(w, col):
        return w[:, col:col + P].reshape(KT, P, P).transpose(1, 0, 2).reshape(P, BLOCK)

    def wide_block(w, k, col):
        return w[k * P:(k + 2) * P, col:col + HALF].reshape(2, P, HALF).transpose(1, 0, 2).reshape(P, BLOCK)

    w_in = np.asarray(inputs["w_in_a"])[0]
    w_out = np.asarray(inputs["w_out"])[0]
    w_kv = np.asarray(inputs["w_mem_kv"])[0]
    b_col, c_col, u_col, gate_col, q_col = 0, D, 2 * D, 3 * D, 3 * D + BR
    order = [proj_block(w_kv, m * P) for m in range(MH)]
    order += [wide_block(w_kv, k, MH * HD) for k in range(0, KT, 2)]
    for h in range(MH):
        order.append(proj_block(w_in, q_col + h * P))
        for j in (2 * h, 2 * h + 1):
            order += [proj_block(w_in, col + j * P) for col in (c_col, u_col, b_col, gate_col)]
        order.append(proj_block(w_in, gate_col + D + h * P))
    for col in (0, HALF):
        order += [wide_block(w_out, k, col) for k in range(0, BT, 2)]

    ins = {
        "x": np.asarray(inputs["x"])[0],
        "x_t": np.asarray(inputs["x"])[0].reshape(NT, TILE, KT, P).transpose(0, 3, 2, 1),
        "mem": np.asarray(inputs["mem"])[0].reshape(NM, KT, P).transpose(2, 1, 0),
        "in_gains": np.stack([np.asarray(inputs[g])[0].reshape(KT, P).T for g in ("pre_norm", "mem_norm")], axis=1),
        "post_g": np.repeat(np.asarray(inputs["post_norm"]).reshape(1, D), P, axis=0),
        "conv": np.asarray(inputs["conv_a"])[0].reshape(CONV, CH, P).transpose(2, 1, 0),
        "blocks": np.stack(order),
    }
    nc = bacc.Bacc("TRN2", target_bir_lowering=False, num_devices=1)
    arrays, args = {}, []
    for name, a in ins.items():
        arrays[f"in_{name}"] = np.ascontiguousarray(a)
        args.append(nc.dram_tensor(f"in_{name}", list(a.shape), mybir.dt.from_np(a.dtype), kind="ExternalInput").ap())
    out = nc.dram_tensor("out_x", [SEQ, D], mybir.dt.float32, kind="ExternalOutput").ap()
    trunk(nc, *args, out)
    r = run_bass_kernel_spmd(nc, [arrays], core_ids=[0])
    return np.asarray(r.results[0]["out_x"]).reshape(1, SEQ, D)
```

```python
from contextlib import ExitStack

import concourse.bass as bass
from concourse import mybir

P = 128
D = 1024
SEQ = 4096
TILE = 512
NT = SEQ // TILE
SUB = TILE // P
KT = D // P
CH = D // P
CONV = 3
HALO = CONV - 1
MH = 4
HD = 128
NM = 256
MT = NM // P
BR = D + MH * HD
BT = BR // P
HALF = 512
PAIRS = KT // 2
MPAIRS = 2
BLOCK = 1024
NKV = 2 * MH * HD * D // (P * BLOCK)
HEAD_BLOCKS = 2 + 2 * 4
PAIR_BLOCKS = 2 * HEAD_BLOCKS
IN_BLOCKS = MH * HEAD_BLOCKS
OUT_BLOCKS = BT * D // BLOCK
TILE_BLOCKS = IN_BLOCKS + OUT_BLOCKS
AHEAD = 3
RING = AHEAD + 1
RES = 3
EPS = 1e-6
SCALE = HD ** -0.5
CREDIT = 2
Q, C0, U0, B0, G0, C1, U1, B1, G1, MG = range(HEAD_BLOCKS)


def trunk(nc, x, x_t, mem, in_gains, post_g, conv, blocks, out):
    f32 = mybir.dt.float32
    f32r = mybir.dt.float32r
    ALU = mybir.AluOpType
    ACT = mybir.ActivationFunctionType
    AX = mybir.AxisListType
    ds = bass.ds

    with ExitStack() as ctx:
        def sb(name, shape, dt=f32):
            return ctx.enter_context(nc.sbuf_tensor(name, [P] + list(shape), dt))

        def sem(name):
            return ctx.enter_context(nc.semaphore(name))

        w_raw = sb("w_raw", [RING, BLOCK])
        w_hi = sb("w_hi", [RING, BLOCK], f32r)
        w_lo = sb("w_lo", [RING, BLOCK], f32r)
        h_hi = sb("h_hi", [KT, TILE], f32r)
        h_lo = sb("h_lo", [KT, TILE], f32r)
        g_hi = sb("g_hi", [BT, TILE], f32r)
        g_lo = sb("g_lo", [BT, TILE], f32r)
        k_hi = sb("k_hi", [MH, NM], f32r)
        k_lo = sb("k_lo", [MH, NM], f32r)
        v_hi = sb("v_hi", [MT, MH * HD], f32r)
        v_lo = sb("v_lo", [MT, MH * HD], f32r)
        vh_hi = sb("vh_hi", [MT, HD], f32r)
        vh_lo = sb("vh_lo", [MT, HD], f32r)
        q_hi = sb("q_hi", [TILE], f32r)
        q_lo = sb("q_lo", [TILE], f32r)
        pt_hi = sb("pt_hi", [MT, TILE], f32r)
        pt_lo = sb("pt_lo", [MT, TILE], f32r)
        x_in = sb("x_in", [KT, TILE])
        x_res = sb("x_res", [RES, D])
        last_rows = x_in[:, 0:D // TILE, :].rearrange("p a b -> p (a b)")
        mem_in = x_res[:, 0:2, :].rearrange("p a (k m) -> p (a k) m", m=NM)
        gains = sb("gains", [2, KT])
        post_gain = sb("post_gain", [D])
        y_left = sb("y_left", [SUB, HALF])
        probs = y_left[:, 0:2, :].rearrange("p a (b m) -> p (a b) m", b=2)
        squares = y_left[:].rearrange("p a b -> p (a b)")
        ones = sb("ones", [P])
        conv_w = sb("conv_w", [CH, CONV])
        z_halo = sb("z_halo", [CH, HALO])
        z = sb("z", [HALO + TILE])
        mix = sb("mix", [TILE])
        scratch = sb("scratch", [2 * TILE])
        c_sb = scratch[:, 0:TILE]
        silu = scratch[:, TILE:]
        sq_sum = scratch[:, :]
        junk = scratch[:, 0:HALF]
        rs_all = z[:, 0:TILE]
        ident = sb("ident", [P])
        eps = sb("eps", [1])
        ysq = sb("ysq", [2, SUB])
        y_left_ms = sb("y_left_ms", [SUB])
        ysd = sb("ysd", [SUB])
        yrs = sb("yrs", [SUB])
        rmax = sb("rmax", [SUB])
        nmax = sb("nmax", [SUB])
        rsum = sb("rsum", [SUB])
        rinv = sb("rinv", [SUB])

        psum = ctx.enter_context(nc.psum_tensor("banks", [P, 8, HALF], f32))
        scores = psum[:, 4:6, :].rearrange("p a (b m) -> p (a b) m", b=2)
        probs_t = psum[:, 6:8, :]
        mem_o = psum[:, 4, :]

        token_sums = psum[:, 5, :]

        w_in_dma = [sem(f"w_in_dma{i}") for i in range(RING)]
        x_in_dma = sem("x_in_dma")
        x_res_dma = [sem(f"x_res_dma{i}") for i in range(RES)]
        out_dma = [sem(f"out_dma{i}") for i in range(RES)]
        mem_dma = sem("mem_dma")
        gains_dma = sem("gains_dma")
        post_dma = sem("post_dma")
        consts_set = sem("consts_set")
        pool_passed = sem("pool_passed")
        w_hi_done = sem("w_hi_done")
        w_lo_done = sem("w_lo_done")
        blocks_done = sem("blocks_done")
        sq_done = sem("sq_done")
        sq_added = sem("sq_added")
        sums_done = sem("sums_done")
        sd_done = sem("sd_done")
        rs_done = sem("rs_done")
        normed = sem("normed")
        h_hi_done = sem("h_hi_done")
        h_lo_done = sem("h_lo_done")
        kv_hi_done = sem("kv_hi_done")
        kv_lo_done = sem("kv_lo_done")
        vh_done = sem("vh_done")
        q_hi_done = sem("q_hi_done")
        q_lo_done = sem("q_lo_done")
        scores_done = sem("scores_done")
        rmax_done = sem("rmax_done")
        nmax_done = sem("nmax_done")
        exp_done = sem("exp_done")
        rinv_done = sem("rinv_done")
        probs_done = sem("probs_done")
        turned_done = sem("turned_done")
        pt_hi_done = sem("pt_hi_done")
        pt_lo_done = sem("pt_lo_done")
        pv_done = sem("pv_done")
        c_done = sem("c_done")
        halo_in = sem("halo_in")
        z_done = sem("z_done")
        halo_out = sem("halo_out")
        tap2_done = sem("tap2_done")
        tap1_done = sem("tap1_done")
        tap0_done = sem("tap0_done")
        b_used = sem("b_used")
        silu_done = sem("silu_done")
        gated = sem("gated")
        g_hi_done = sem("g_hi_done")
        g_lo_done = sem("g_lo_done")
        y_left_done = sem("y_left_done")
        y_right_done = sem("y_right_done")
        ysq_done = sem("ysq_done")
        left_done = sem("left_done")
        ysd_done = sem("ysd_done")
        yrs_done = sem("yrs_done")
        y_scaled = sem("y_scaled")
        y_final = sem("y_final")

        block = ctx.enter_context(nc.Block())

        def per_tile(i):
            return len(range(i, SUB, RES))

        def flat(ap):
            return ap.rearrange("p a b -> p (a b)")

        @block.sync
        def _(sp):
            def load(slot, src):
                sp.dma_start(w_raw[:, slot, :], src).then_inc(w_in_dma[slot], 16)

            sp.dma_start(mem_in, mem).then_inc(mem_dma, 16)
            for m in range(NKV):
                if m >= RING:
                    sp.wait_ge(w_lo_done, m - RING + 1)
                load(m % RING, blocks[m])
            with sp.Fori(0, NT) as t:
                with sp.Fori(0, TILE_BLOCKS // RING) as turn:
                    for i in range(RING):
                        m = NKV + t * TILE_BLOCKS + turn * RING + i
                        sp.wait_ge(w_lo_done, m - RING + 1)
                        src = blocks[ds(NKV + turn * RING + i, 1), :, :].rearrange("a p n -> p (a n)")
                        load(i, src)

        @block.gpsimd
        def _(pool):
            pool.dma_start(gains[:], in_gains).then_inc(gains_dma, 16)
            pool.dma_start(x_in[:], x_t[0]).then_inc(x_in_dma, 16)
            pool.dma_start(conv_w[:], conv).then_inc(post_dma, 16)
            pool.dma_start(post_gain[:], post_g).then_inc(post_dma, 16)
            pool.memset(ones[:], 1.0).then_inc(consts_set, 1)
            pool.memset(eps[:], EPS).then_inc(consts_set, 1)
            pool.memset(z_halo[:], 0.0).then_inc(consts_set, 1)
            pool.memset(ident[:], 0.0).then_inc(consts_set, 1)
            pool.wait_ge(consts_set, 4)
            pool.affine_select(out=ident[:], in_=ident[:], compare_op=ALU.not_equal, fill=1.0, base=0,
                               pattern=[[-1, P]], channel_multiplier=1).then_inc(consts_set, 1)

            def load_residual(t, s):
                pool.dma_start(x_res[:, s % RES, :], x[ds((t * SUB + s) * P, P), :]).then_inc(x_res_dma[s % RES], 16)

            def tile(t, more):
                for s in range(RES):
                    load_residual(t, s)
                pool.wait_ge(h_lo_done, MPAIRS + (t + 1) * PAIRS)
                if not more:
                    pool.dma_start(last_rows, x[(NT * SUB - 1) * P:, :]).then_inc(x_in_dma, 16)
                else:
                    pool.sem_inc(pool_passed, 1)
                    pool.dma_start(x_in[:], x_t[ds(t + 1, 1)].rearrange("a p k n -> p (a k) n")).then_inc(x_in_dma, 16)
                for s in range(SUB):
                    pool.wait_ge(y_final, CREDIT + t * SUB + s + 1)
                    pool.sem_inc(pool_passed, 1)
                    rows = last_rows if not more and s >= RES else x_res[:, s % RES, :]
                    pool.dma_start(out[ds((t * SUB + s) * P, P), :], rows).then_inc(out_dma[s % RES], 16)
                    if more and s + RES < SUB:
                        pool.wait_ge(out_dma[s], (t * 2 + 1) * 16)
                        pool.sem_inc(pool_passed, 1)
                        load_residual(t, s + RES)
                for i in range(RES):
                    pool.wait_ge(out_dma[i], (t + 1) * per_tile(i) * 16)

            pool.wait_ge(h_lo_done, MPAIRS)
            with pool.Fori(0, NT - 1) as t:
                tile(t, True)
            tile(NT - 1, False)

        @block.scalar
        def _(act):
            def hi_of(turn, i):
                slot = i % RING
                act.wait_ge(w_in_dma[slot], (turn + i // RING + 1) * 16)
                act.wait_ge(blocks_done, turn * RING + i - RING + 1)
                nc.scalar.activation(w_hi[:, slot, :], w_raw[:, slot, :], ACT.Copy).then_inc(w_hi_done, 1)

            def square(which, src):
                act.wait_ge(sq_added, which)
                nc.scalar.activation(squares, flat(src), ACT.Square).then_inc(sq_done, 1)

            def root(nth, dst, src):
                act.wait_ge(sums_done, nth)
                nc.scalar.activation(dst, src, ACT.Sqrt, scale=1.0 / D, bias=eps[:]).then_inc(sd_done, 1)

            def hi_of_pair(tile, a):
                act.wait_ge(normed, (tile + 1) * KT + 2 * a + 2)
                nc.scalar.activation(h_hi[:, 2 * a:2 * a + 2, :], x_in[:, 2 * a:2 * a + 2, :], ACT.Copy).then_inc(h_hi_done, 1)

            def first_hi(m):
                act.wait_ge(w_in_dma[m % RING], (m // RING + 1) * 16)
                if m >= RING:
                    act.wait_ge(blocks_done, m - RING + 1)
                nc.scalar.activation(w_hi[:, m % RING, :], w_raw[:, m % RING, :], ACT.Copy).then_inc(w_hi_done, 1)

            act.sem_inc(silu_done, CREDIT)
            act.wait_ge(mem_dma, 16)
            nc.scalar.activation(squares, flat(mem_in), ACT.Square).then_inc(sq_done, 1)
            act.wait_ge(consts_set, 5)
            first_hi(0)
            first_hi(1)
            root(1, rs_all[:, 0:NM], token_sums[:, 0:NM])
            first_hi(2)
            for a in range(MPAIRS):
                ks = slice(a * KT // 2, (a + 1) * KT // 2)
                act.wait_ge(normed, (a + 1) * KT // 2)
                nc.scalar.activation(g_hi[:, ks, 0:NM], mem_in[:, ks, :], ACT.Copy).then_inc(h_hi_done, 1)
            act.wait_ge(x_in_dma, 16)
            square(3, x_in[:, 0:KT // 2, :])
            square(4, x_in[:, KT // 2:, :])
            for m in range(NKV):
                first_hi(m + AHEAD)
                if 1 <= m <= MH:
                    act.wait_ge(blocks_done, m)
                    nc.scalar.activation(k_hi[:, m - 1, :], psum[:, m - 1, 0:NM], ACT.Copy).then_inc(kv_hi_done, 1)
                if m == 1:
                    root(2, rs_all, token_sums)
                if 2 <= m < 2 + PAIRS:
                    hi_of_pair(0, m - 2)
            act.wait_ge(blocks_done, NKV)
            for m in range(MT):
                nc.scalar.activation(v_hi[:, m, :], psum[:, 6 + m, :], ACT.Copy).then_inc(kv_hi_done, 1)

            def head_step(t, hp, i):
                h = t * MH + hp * 2 + i
                j = h * 2
                turn = NKV // RING + t * (TILE_BLOCKS // RING) + hp * (PAIR_BLOCKS // RING)
                n = NKV + t * TILE_BLOCKS + hp * PAIR_BLOCKS + i * HEAD_BLOCKS

                def ahead(p):
                    hi_of(turn, i * HEAD_BLOCKS + p + AHEAD)

                def came(p):
                    act.wait_ge(blocks_done, n + p + 1)

                def gate(p, bank, item):
                    came(p)
                    act.wait_ge(gated, CREDIT + h * 3 + item)
                    nc.scalar.activation(silu, psum[:, bank, :], ACT.Silu).then_inc(silu_done, 1)

                def hi_of_gated(item, dst):
                    act.wait_ge(gated, CREDIT + h * 3 + item + 1)
                    nc.scalar.activation(dst, mix[:], ACT.Copy).then_inc(g_hi_done, 1)

                ahead(Q)
                came(Q)
                nc.scalar.activation(q_hi[:], psum[:, 0, :], ACT.Copy).then_inc(q_hi_done, 1)
                ahead(C0)
                came(C0)
                act.wait_ge(z_done, CREDIT + j)
                nc.scalar.activation(c_sb, psum[:, 1, :], ACT.Copy).then_inc(c_done, 1)
                ahead(U0)
                ahead(B0)
                ahead(G0)
                act.wait_ge(nmax_done, h + 1)
                if i == 0:
                    act.wait_ge(y_final, CREDIT + t * SUB)
                for s in range(SUB):
                    op = nc.scalar.activation(probs[:, s, :], scores[:, s, :], ACT.Exp, scale=SCALE,
                                              bias=nmax[:, s:s + 1], accum_out=rsum[:, s:s + 1])
                    op.then_inc(exp_done, 1)
                gate(G0, 0, 0)
                ahead(C1)
                hi_of_gated(0, flat(g_hi[:, ds(hp * 4 + i * 2, 1), :]))
                came(C1)
                act.wait_ge(z_done, CREDIT + j + 1)
                nc.scalar.activation(c_sb, psum[:, 1, :], ACT.Copy).then_inc(c_done, 1)
                ahead(U1)
                ahead(B1)
                act.wait_ge(turned_done, h + 1)
                nc.scalar.activation(flat(pt_hi[:]), flat(probs_t), ACT.Copy).then_inc(pt_hi_done, 1)
                ahead(G1)
                gate(G1, 0, 1)
                ahead(MG)
                hi_of_gated(1, flat(g_hi[:, ds(hp * 4 + i * 2 + 1, 1), :]))
                gate(MG, 3, 2)
                hi_of_gated(2, flat(g_hi[:, ds(hp * 2 + i + CH, 1), :]))

            def out_step(t, more):
                n = NKV + t * TILE_BLOCKS + IN_BLOCKS
                turn = (NKV + IN_BLOCKS) // RING + t * (TILE_BLOCKS // RING)
                nth = t + 1
                for p in range(OUT_BLOCKS):
                    if more or p + AHEAD < OUT_BLOCKS:
                        hi_of(turn, p + AHEAD)
                    if more and p == 0:
                        act.wait_ge(x_in_dma, (nth + 1) * 16)
                        act.wait_ge(turned_done, (t + 1) * MH)
                        square(3 + nth * 4, x_in[:, 0:KT // 2, :])
                    if more and p == 1:
                        square(4 + nth * 4, x_in[:, KT // 2:, :])
                    if more and p == 4:
                        root(nth + 2, rs_all, token_sums)
                    if more and 5 <= p < 5 + PAIRS:
                        hi_of_pair(nth, p - 5)
                    if p == OUT_BLOCKS // 2:
                        act.wait_ge(blocks_done, n + p)
                        for s in range(SUB):
                            if s:
                                act.wait_ge(ysq_done, t * 2 * SUB + s)
                            nc.scalar.activation(junk, psum[:, s, :], ACT.Square,
                                                 accum_out=ysq[:, 0, s:s + 1]).then_inc(ysq_done, 1)
                act.wait_ge(left_done, t + 1)
                for s in range(SUB):
                    if s < SUB - 1:
                        act.wait_ge(y_right_done, t * (SUB - 1) + s + 1)
                    else:
                        act.wait_ge(blocks_done, n + OUT_BLOCKS)
                    act.wait_ge(ysq_done, t * 2 * SUB + SUB + s)
                    nc.scalar.activation(junk, psum[:, 4 + s, :], ACT.Square,
                                         accum_out=ysq[:, 1, s:s + 1]).then_inc(ysq_done, 1)
                    act.wait_ge(ysq_done, t * 2 * SUB + SUB + s + 1)
                    nc.scalar.activation(ysd[:, s:s + 1], ysq[:, 1, s:s + 1], ACT.Sqrt, scale=1.0 / D,
                                         bias=y_left_ms[:, s:s + 1]).then_inc(ysd_done, 1)

            with act.Fori(0, NT - 1) as t:
                with act.Fori(0, MH // 2) as hp:
                    for i in range(2):
                        head_step(t, hp, i)
                out_step(t, True)
            with act.Fori(0, MH // 2) as hp:
                for i in range(2):
                    head_step(NT - 1, hp, i)
            out_step(NT - 1, False)

        @block.vector
        def _(dve):
            def lo_of(m, slot):
                dve.wait_ge(w_hi_done, m + 1)
                nc.vector.tensor_tensor(w_lo[:, slot, :], w_raw[:, slot, :], w_hi[:, slot, :].bitcast(f32),
                                        ALU.subtract).then_inc(w_lo_done, 1)

            def inverse(nth, n):
                dve.wait_ge(sd_done, nth)
                nc.vector.reciprocal(rs_all[:, 0:n], rs_all[:, 0:n]).then_inc(rs_done, 1)
                dve.wait_ge(rs_done, nth)

            def norm(rows, k, which, n):
                nc.vector.scalar_tensor_tensor(out=rows[:, k, :], in0=rows[:, k, :], scalar=gains[:, which, k:k + 1],
                                               in1=rs_all[:, 0:n], op0=ALU.mult, op1=ALU.mult).then_inc(normed, 1)

            def norm_pair(a):
                for k in (2 * a, 2 * a + 1):
                    norm(x_in, k, 0, TILE)

            def lo_of_pair(tile, a):
                dve.wait_ge(h_hi_done, MPAIRS + tile * PAIRS + a + 1)
                ks = slice(2 * a, 2 * a + 2)
                nc.vector.tensor_tensor(h_lo[:, ks, :], x_in[:, ks, :], h_hi[:, ks, :].bitcast(f32),
                                        ALU.subtract).then_inc(h_lo_done, 1)

            def add_squares(tile, half):
                before = 3 + tile * 4
                dve.wait_ge(sq_done, 1 + tile * 2 + half + 1)
                if not half:
                    dve.wait_ge(sq_added, before)
                    nc.vector.tensor_tensor(sq_sum, squares[:, 0:2 * TILE], squares[:, 2 * TILE:], ALU.add).then_inc(sq_added, 1)
                    return
                for i in range(2):
                    dve.wait_ge(sq_added, before + 1 + i)
                    nc.vector.tensor_tensor(sq_sum, squares[:, i * 2 * TILE:(i + 1) * 2 * TILE], sq_sum,
                                            ALU.add).then_inc(sq_added, 1)
                dve.wait_ge(sq_added, before + 3)
                nc.vector.tensor_tensor(sq_sum[:, 0:TILE], sq_sum[:, 0:TILE], sq_sum[:, TILE:], ALU.add).then_inc(sq_added, 1)

            for credited in (z_done, b_used, gated, g_lo_done, y_final):
                dve.sem_inc(credited, CREDIT)
            dve.wait_ge(sq_done, 1)
            nc.vector.tensor_tensor(sq_sum, squares[:, 0:4 * NM], squares[:, 4 * NM:], ALU.add).then_inc(sq_added, 1)
            for i, n in ((1, 2 * NM), (2, NM)):
                dve.wait_ge(sq_added, i)
                nc.vector.tensor_tensor(sq_sum[:, 0:n], sq_sum[:, 0:n], sq_sum[:, n:2 * n], ALU.add).then_inc(sq_added, 1)
            lo_of(0, 0)
            lo_of(1, 1)
            dve.wait_ge(gains_dma, 16)
            inverse(1, NM)
            for k in range(KT):
                norm(mem_in, k, 1, NM)
            for a in range(MPAIRS):
                ks = slice(a * KT // 2, (a + 1) * KT // 2)
                dve.wait_ge(h_hi_done, a + 1)
                nc.vector.tensor_tensor(g_lo[:, ks, 0:NM], mem_in[:, ks, :], g_hi[:, ks, 0:NM].bitcast(f32),
                                        ALU.subtract).then_inc(h_lo_done, 1)
            add_squares(0, 0)
            lo_of(2, 2)
            add_squares(0, 1)
            for m in range(NKV):
                lo_of(m + AHEAD, (m + AHEAD) % RING)
                if 1 <= m <= MH:
                    dve.wait_ge(kv_hi_done, m)
                    nc.vector.tensor_tensor(k_lo[:, m - 1, :], psum[:, m - 1, 0:NM], k_hi[:, m - 1, :].bitcast(f32),
                                            ALU.subtract).then_inc(kv_lo_done, 1)
                if m == 1:
                    inverse(2, TILE)
                if 1 <= m < 1 + PAIRS:
                    norm_pair(m - 1)
                if 2 <= m < 2 + PAIRS:
                    lo_of_pair(0, m - 2)
            for m in range(MT):
                dve.wait_ge(kv_hi_done, MH + m + 1)
                nc.vector.tensor_tensor(v_lo[:, m, :], psum[:, 6 + m, :], v_hi[:, m, :].bitcast(f32),
                                        ALU.subtract).then_inc(kv_lo_done, 1)
            dve.wait_ge(kv_lo_done, MH + MT)
            dve.wait_ge(post_dma, 32)

            def head_step(t, hp, i):
                h = t * MH + hp * 2 + i
                n = NKV + t * TILE_BLOCKS + hp * PAIR_BLOCKS + i * HEAD_BLOCKS

                def ahead(p):
                    a = i * HEAD_BLOCKS + p + AHEAD
                    lo_of(n + p + AHEAD, a % RING)

                def came(p):
                    dve.wait_ge(blocks_done, n + p + 1)

                def make_z(p, jj):
                    j = h * 2 + jj
                    own = hp * 4 + i * 2 + jj
                    halo = flat(z_halo[:, ds(own, 1), :])
                    dve.wait_ge(b_used, CREDIT + j)
                    nc.vector.tensor_scalar(z[:, 0:HALO], halo, 1.0, None, ALU.mult).then_inc(halo_in, 1)
                    came(p)
                    dve.wait_ge(c_done, j + 1)
                    nc.vector.tensor_tensor(z[:, HALO:], psum[:, 2, :], c_sb, ALU.mult).then_inc(z_done, 1)
                    dve.wait_ge(halo_in, j + 1)
                    dve.wait_ge(z_done, CREDIT + j + 1)
                    nc.vector.tensor_scalar(halo, z[:, TILE:TILE + HALO], 1.0, None, ALU.mult).then_inc(halo_out, 1)

                def convolve(p, jj):
                    j = h * 2 + jj
                    dve.wait_ge(halo_out, j + 1)
                    w = flat(conv_w[:, ds(hp * 4 + i * 2 + jj, 1), :])
                    dve.wait_ge(g_lo_done, CREDIT + h * 3 + jj)
                    nc.vector.tensor_scalar(mix[:], z[:, 2:2 + TILE], w[:, 2:3], None, ALU.mult).then_inc(tap2_done, 1)
                    dve.wait_ge(tap2_done, j + 1)
                    nc.vector.scalar_tensor_tensor(out=mix[:], in0=z[:, 1:1 + TILE], scalar=w[:, 1:2], in1=mix[:],
                                                   op0=ALU.mult, op1=ALU.add).then_inc(tap1_done, 1)
                    dve.wait_ge(tap1_done, j + 1)
                    nc.vector.scalar_tensor_tensor(out=mix[:], in0=z[:, 0:TILE], scalar=w[:, 0:1], in1=mix[:],
                                                   op0=ALU.mult, op1=ALU.add).then_inc(tap0_done, 1)
                    came(p)
                    dve.wait_ge(tap0_done, j + 1)
                    nc.vector.tensor_tensor(mix[:], psum[:, 3, :], mix[:], ALU.mult).then_inc(b_used, 1)

                def gate_it(item, silu_n, src, at):
                    dve.wait_ge(silu_done, silu_n)
                    nc.vector.tensor_tensor(mix[:], src, silu, ALU.mult).then_inc(gated, 1)
                    dve.wait_ge(g_hi_done, h * 3 + item + 1)
                    nc.vector.tensor_tensor(flat(g_lo[:, ds(at, 1), :]), mix[:],
                                            flat(g_hi[:, ds(at, 1), :]).bitcast(f32), ALU.subtract).then_inc(g_lo_done, 1)

                ahead(Q)
                dve.wait_ge(q_hi_done, h + 1)
                nc.vector.tensor_tensor(q_lo[:], psum[:, 0, :], q_hi[:].bitcast(f32), ALU.subtract).then_inc(q_lo_done, 1)
                ahead(C0)
                for src, dst in ((v_hi, vh_hi), (v_lo, vh_lo)):
                    nc.vector.tensor_scalar(dst[:], src[:, :, ds((hp * 2 + i) * HD, HD)].bitcast(f32), 1.0, None,
                                            ALU.mult).then_inc(vh_done, 1)
                ahead(U0)
                make_z(U0, 0)
                ahead(B0)
                dve.wait_ge(scores_done, h + 1)
                nc.vector.tensor_reduce(rmax[:], scores, AX.X, ALU.max).then_inc(rmax_done, 1)
                dve.wait_ge(rmax_done, h + 1)
                nc.vector.tensor_scalar(nmax[:], rmax[:], -SCALE, None, ALU.mult).then_inc(nmax_done, 1)
                ahead(G0)
                convolve(B0, 0)
                dve.wait_ge(exp_done, (h + 1) * SUB)
                nc.vector.reciprocal(rinv[:], rsum[:]).then_inc(rinv_done, 1)
                dve.wait_ge(rinv_done, h + 1)
                for s in range(SUB):
                    nc.vector.tensor_scalar(probs[:, s, :], probs[:, s, :], rinv[:, s:s + 1], None,
                                            ALU.mult).then_inc(probs_done, 1)
                ahead(C1)
                dve.wait_ge(b_used, CREDIT + h * 2 + 1)
                gate_it(0, CREDIT + h * 3 + 1, mix[:], hp * 4 + i * 2)
                ahead(U1)
                make_z(U1, 1)
                ahead(B1)
                dve.wait_ge(pt_hi_done, h + 1)
                nc.vector.tensor_tensor(flat(pt_lo[:]), flat(probs_t), flat(pt_hi[:]).bitcast(f32),
                                        ALU.subtract).then_inc(pt_lo_done, 1)
                convolve(B1, 1)
                ahead(G1)
                dve.wait_ge(b_used, CREDIT + h * 2 + 2)
                gate_it(1, CREDIT + h * 3 + 2, mix[:], hp * 4 + i * 2 + 1)
                ahead(MG)
                dve.wait_ge(pv_done, h + 1)
                dve.wait_ge(g_lo_done, CREDIT + h * 3 + 2)
                gate_it(2, CREDIT + h * 3 + 3, mem_o, hp * 2 + i + CH)

            def out_step(t, more):
                n = NKV + t * TILE_BLOCKS + IN_BLOCKS
                nth = t + 1
                for p in range(OUT_BLOCKS):
                    if more or p + AHEAD < OUT_BLOCKS:
                        lo_of(n + p + AHEAD, (p + AHEAD) % RING)
                    if more and p < 2:
                        add_squares(nth, p)
                    if more and p == 4:
                        inverse(nth + 2, TILE)
                    if more and 5 <= p < 5 + PAIRS:
                        norm_pair(p - 5)
                        lo_of_pair(nth, p - 5)
                    if p == OUT_BLOCKS // 2:
                        for s in range(SUB):
                            dve.wait_ge(ysq_done, t * 2 * SUB + s + 1)
                            nc.vector.tensor_tensor(y_left[:, s, :], psum[:, s, :], post_gain[:, 0:HALF],
                                                    ALU.mult).then_inc(y_left_done, 1)
                        nc.vector.tensor_scalar(y_left_ms[:], ysq[:, 0, :], 1.0 / D, EPS, ALU.mult,
                                                ALU.add).then_inc(left_done, 1)
                for s in range(SUB):
                    i = s % RES
                    kept = not more and s >= RES
                    rows = last_rows if kept else x_res[:, i, :]
                    left, right = rows[:, 0:HALF], rows[:, HALF:]
                    y_right = psum[:, 4 + s, :]
                    dve.wait_ge(ysd_done, t * SUB + s + 1)
                    nc.vector.reciprocal(yrs[:, s:s + 1], ysd[:, s:s + 1]).then_inc(yrs_done, 1)
                    dve.wait_ge(yrs_done, t * SUB + s + 1)
                    nc.vector.scalar_tensor_tensor(out=y_right, in0=y_right, scalar=yrs[:, s:s + 1],
                                                   in1=post_gain[:, HALF:], op0=ALU.mult, op1=ALU.mult).then_inc(y_scaled, 1)
                    if kept:
                        dve.wait_ge(x_in_dma, (NT + 1) * 16)
                    else:
                        dve.wait_ge(x_res_dma[i], (t * per_tile(i) + s // RES + 1) * 16)
                    dve.wait_ge(y_left_done, t * SUB + s + 1)
                    nc.vector.scalar_tensor_tensor(out=left, in0=y_left[:, s, :], scalar=yrs[:, s:s + 1], in1=left,
                                                   op0=ALU.mult, op1=ALU.add)
                    dve.wait_ge(y_scaled, t * SUB + s + 1)
                    nc.vector.tensor_tensor(right, y_right, right, ALU.add).then_inc(y_final, 1)

            with dve.Fori(0, NT - 1) as t:
                with dve.Fori(0, MH // 2) as hp:
                    for i in range(2):
                        head_step(t, hp, i)
                out_step(t, True)
            with dve.Fori(0, MH // 2) as hp:
                for i in range(2):
                    head_step(NT - 1, hp, i)
            out_step(NT - 1, False)

        @block.tensor
        def _(pe):
            def product(dst, left, right, first, last):
                (a, b), (c, d) = left, right
                nc.tensor.matmul(dst, a, c, start=first, stop=False)
                nc.tensor.matmul(dst, a, d, start=False, stop=False)
                return nc.tensor.matmul(dst, b, c, start=False, stop=last)

            def sum_tokens(n, count):
                pe.wait_ge(sq_added, count)
                nc.tensor.matmul(token_sums[:, 0:n], ones[:], sq_sum[:, 0:n], start=True, stop=True).then_inc(sums_done, 1)

            pe.wait_ge(consts_set, 5)
            sum_tokens(NM, 3)
            for m in range(MH):
                pe.wait_ge(w_lo_done, m + 1)
                for k in range(KT):
                    if m == 0 and k % (KT // MPAIRS) == 0:
                        pe.wait_ge(h_lo_done, k // (KT // MPAIRS) + 1)
                    w = [a[:, m % RING, k * P:(k + 1) * P] for a in (w_hi, w_lo)]
                    op = product(psum[:, m, 0:NM], w, [a[:, k, 0:NM] for a in (g_hi, g_lo)], k == 0, k == KT - 1)
                op.then_inc(blocks_done, 1)
                if m == 1:
                    sum_tokens(TILE, 3 + 4)
            for m in range(MH, NKV):
                pe.wait_ge(w_lo_done, m + 1)
                for kk in range(2):
                    k = (m - MH) * 2 + kk
                    for a in range(MT):
                        rows = [u[:, k, a * P:(a + 1) * P] for u in (g_hi, g_lo)]
                        w = [u[:, m % RING, kk * HALF:(kk + 1) * HALF] for u in (w_hi, w_lo)]
                        op = product(psum[:, 6 + a, :], rows, w, k == 0, k == KT - 1)
                op.then_inc(blocks_done, 1)
            pe.wait_ge(kv_lo_done, MH)
            pe.wait_ge(h_lo_done, MPAIRS + PAIRS)

            def head_step(t, hp, i):
                h = t * MH + hp * 2 + i
                j = h * 2
                n = NKV + t * TILE_BLOCKS + hp * PAIR_BLOCKS + i * HEAD_BLOCKS

                def project(p, bank):
                    slot = (i * HEAD_BLOCKS + p) % RING
                    pe.wait_ge(w_lo_done, n + p + 1)
                    for k in range(KT):
                        w = [a[:, slot, k * P:(k + 1) * P] for a in (w_hi, w_lo)]
                        op = product(psum[:, bank, :], w, [a[:, k, :] for a in (h_hi, h_lo)], k == 0, k == KT - 1)
                    op.then_inc(blocks_done, 1)

                pe.wait_ge(silu_done, CREDIT + h * 3 - 1)
                project(Q, 0)
                project(C0, 1)
                pe.wait_ge(z_done, CREDIT + j)
                project(U0, 2)
                pe.wait_ge(silu_done, CREDIT + h * 3)
                project(B0, 3)
                pe.wait_ge(q_lo_done, h + 1)
                pe.wait_ge(g_lo_done, CREDIT + h * 3)
                pe.wait_ge(y_final, CREDIT + t * SUB)
                head = hp * 2 + i
                keys = [flat(a[:, ds(head, 1), :]) for a in (k_hi, k_lo)]
                for s in range(SUB):
                    op = product(scores[:, s, :], [a[:, s * P:(s + 1) * P] for a in (q_hi, q_lo)], keys, True, True)
                op.then_inc(scores_done, 1)
                project(G0, 0)
                pe.wait_ge(c_done, j + 1)
                project(C1, 1)
                pe.wait_ge(z_done, CREDIT + j + 1)
                project(U1, 2)
                pe.wait_ge(probs_done, (h + 1) * SUB)
                for s in range(SUB):
                    for a in range(MT):
                        op = nc.tensor.transpose(probs_t[:, a, s * P:(s + 1) * P], probs[:, s, a * P:(a + 1) * P], ident[:])
                op.then_inc(turned_done, 1)
                pe.wait_ge(b_used, CREDIT + j + 1)
                project(B1, 3)
                pe.wait_ge(silu_done, CREDIT + h * 3 + 1)
                project(G1, 0)
                pe.wait_ge(pt_lo_done, h + 1)
                pe.wait_ge(vh_done, (h + 1) * 2)
                for a in range(MT):
                    op = product(mem_o, [u[:, a, :] for u in (vh_hi, vh_lo)], [u[:, a, :] for u in (pt_hi, pt_lo)],
                                 a == 0, a == MT - 1)
                op.then_inc(pv_done, 1)
                pe.wait_ge(b_used, CREDIT + j + 2)
                project(MG, 3)

            def out_step(t, more):
                n = NKV + t * TILE_BLOCKS + IN_BLOCKS
                nth = t + 1
                pe.wait_ge(silu_done, CREDIT + (t + 1) * MH * 3 - 1)
                pe.wait_ge(z_done, CREDIT + (t + 1) * CH)
                for p in range(OUT_BLOCKS):
                    right, b = divmod(p, OUT_BLOCKS // 2)
                    pe.wait_ge(w_lo_done, n + p + 1)
                    if not right:
                        step = t * MH + (b if b < MH else MH - 1)
                        pe.wait_ge(g_lo_done, CREDIT + step * 3 + (2 if b < MH else 3))
                    for s in range(SUB):
                        for kk in range(2):
                            k = 2 * b + kk
                            g = [a[:, k, s * P:(s + 1) * P] for a in (g_hi, g_lo)]
                            w = [a[:, p % RING, kk * HALF:(kk + 1) * HALF] for a in (w_hi, w_lo)]
                            if k == 0 and not right and s == SUB - 1:
                                pe.wait_ge(silu_done, CREDIT + (t + 1) * MH * 3)
                            if k == 0 and right and s == 1 and more:
                                pe.wait_ge(sd_done, nth + 2)
                            op = product(psum[:, 4 * right + s, :], g, w, k == 0, k == BT - 1)
                            if right and k == BT - 1 and s < SUB - 1:
                                op.then_inc(y_right_done, 1)
                    op.then_inc(blocks_done, 1)
                    if more and p == 3:
                        sum_tokens(TILE, 3 + (nth + 1) * 4)
                pe.wait_ge(y_left_done, (t + 1) * SUB)
                pe.wait_ge(ysq_done, t * 2 * SUB + SUB)
                if more:
                    pe.wait_ge(h_lo_done, MPAIRS + (nth + 1) * PAIRS)

            with pe.Fori(0, NT - 1) as t:
                with pe.Fori(0, MH // 2) as hp:
                    for i in range(2):
                        head_step(t, hp, i)
                out_step(t, True)
            with pe.Fori(0, MH // 2) as hp:
                for i in range(2):
                    head_step(NT - 1, hp, i)
            out_step(NT - 1, False)


def kernel(**inputs):
    import numpy as np
    import concourse.bacc as bacc
    from concourse.bass_utils import run_bass_kernel_spmd

    def proj_block(w, col):
        return w[:, col:col + P].reshape(KT, P, P).transpose(1, 0, 2).reshape(P, BLOCK)

    def wide_block(w, k, col):
        return w[k * P:(k + 2) * P, col:col + HALF].reshape(2, P, HALF).transpose(1, 0, 2).reshape(P, BLOCK)

    w_in = np.asarray(inputs["w_in_a"])[0]
    w_out = np.asarray(inputs["w_out"])[0]
    w_kv = np.asarray(inputs["w_mem_kv"])[0]
    b_col, c_col, u_col, gate_col, q_col = 0, D, 2 * D, 3 * D, 3 * D + BR
    order = [proj_block(w_kv, m * P) for m in range(MH)]
    order += [wide_block(w_kv, k, MH * HD) for k in range(0, KT, 2)]
    for h in range(MH):
        order.append(proj_block(w_in, q_col + h * P))
        for j in (2 * h, 2 * h + 1):
            order += [proj_block(w_in, col + j * P) for col in (c_col, u_col, b_col, gate_col)]
        order.append(proj_block(w_in, gate_col + D + h * P))
    for col in (0, HALF):
        order += [wide_block(w_out, k, col) for k in range(0, BT, 2)]

    ins = {
        "x": np.asarray(inputs["x"])[0],
        "x_t": np.asarray(inputs["x"])[0].reshape(NT, TILE, KT, P).transpose(0, 3, 2, 1),
        "mem": np.asarray(inputs["mem"])[0].reshape(NM, KT, P).transpose(2, 1, 0),
        "in_gains": np.stack([np.asarray(inputs[g])[0].reshape(KT, P).T for g in ("pre_norm", "mem_norm")], axis=1),
        "post_g": np.repeat(np.asarray(inputs["post_norm"]).reshape(1, D), P, axis=0),
        "conv": np.asarray(inputs["conv_a"])[0].reshape(CONV, CH, P).transpose(2, 1, 0),
        "blocks": np.stack(order),
    }
    nc = bacc.Bacc("TRN2", target_bir_lowering=False, num_devices=1)
    arrays, args = {}, []
    for name, a in ins.items():
        arrays[f"in_{name}"] = np.ascontiguousarray(a)
        args.append(nc.dram_tensor(f"in_{name}", list(a.shape), mybir.dt.from_np(a.dtype), kind="ExternalInput").ap())
    out = nc.dram_tensor("out_x", [SEQ, D], mybir.dt.float32, kind="ExternalOutput").ap()
    trunk(nc, *args, out)
    r = run_bass_kernel_spmd(nc, [arrays], core_ids=[0])
    return np.asarray(r.results[0]["out_x"]).reshape(1, SEQ, D)
```
